# Optimizing a Trainium2 kernel written in Bass

```python
import math
import jax
import jax.numpy as jnp
from jax import lax
import numpy as np

D_MODEL = 1024
BATCH = 1
SEQ = 256
DEPTH = 2
DEC_BATCH = 1
DEC_SEQ = 64
PAST_LEN = 512

CHUNK = 64
QBLOCK = 128
HEAD_DIM = 64
GROUP_WIDTH = D_MODEL // 4
N_GH = GROUP_WIDTH // HEAD_DIM
RMS_EPS = 1e-6
ROPE_THETA = 10000.0
LRU_WIDTH = GROUP_WIDTH
LRU_BLOCKS = N_GH
LRU_BLOCK = LRU_WIDTH // LRU_BLOCKS
CONV_W = 4
LRU_C = 8.0
MLA_HEADS = N_GH
MLA_Q_RANK = GROUP_WIDTH
MLA_KV_RANK = GROUP_WIDTH // 2
MLA_NOPE = HEAD_DIM
MLA_ROPE = HEAD_DIM // 2
MLA_V = HEAD_DIM
RET_HEADS = N_GH
RET_DK = HEAD_DIM
RET_DV = HEAD_DIM
MLSTM_HEADS = N_GH
MLSTM_DK = HEAD_DIM
MLSTM_DV = HEAD_DIM
FFN_HIDDEN = -(-8 * D_MODEL // (3 * 256)) * 256

IN_SIZES = (LRU_WIDTH, LRU_WIDTH,
            MLA_Q_RANK, MLA_KV_RANK, MLA_ROPE,
            RET_HEADS * RET_DK, RET_HEADS * RET_DK, RET_HEADS * RET_DV, RET_HEADS * RET_DV,
            MLSTM_HEADS * MLSTM_DK, MLSTM_HEADS * MLSTM_DK, MLSTM_HEADS * MLSTM_DV, MLSTM_HEADS * MLSTM_DV,
            2 * MLSTM_HEADS)
IN_DIM = sum(IN_SIZES)

kernel_name = 'hybrid_parallel_groups_stream_step'

def rms(x, g):
    xf = x.astype(jnp.float32)
    return xf * lax.rsqrt(jnp.mean(xf * xf, axis=-1, keepdims=True) + RMS_EPS) * g

def head_rms(x, g):
    shp = x.shape
    xh = x.reshape(shp[:-1] + (shp[-1] // HEAD_DIM, HEAD_DIM))
    return rms(xh, g.reshape(-1, HEAD_DIM)).reshape(shp)

def rope(x, pos):
    half = x.shape[-1] // 2
    inv = ROPE_THETA ** (-jnp.arange(half, dtype=jnp.float32) / half)
    ang = pos[:, None] * inv[None, :]
    cos = jnp.cos(ang)[None, :, None, :]
    sin = jnp.sin(ang)[None, :, None, :]
    x1, x2 = x[..., :half], x[..., half:]
    return jnp.concatenate([x1 * cos - x2 * sin, x1 * sin + x2 * cos], axis=-1)

def to_chunks(x, L):
    B, T = x.shape[:2]
    return x.reshape((B, T // L, L) + x.shape[2:]).swapaxes(0, 1)

def from_chunks(y):
    n, B, L = y.shape[:3]
    return y.swapaxes(0, 1).reshape((B, n * L) + y.shape[3:])

def causal_conv(x, buf, w, b):
    T = x.shape[1]
    xp = jnp.concatenate([buf.astype(x.dtype), x], axis=1)
    y = b + w[0] * xp[:, 0:T]
    for j in range(1, CONV_W):
        y = y + w[j] * xp[:, j:j + T]
    return y, xp[:, -(CONV_W - 1):]

def rglru(xc, h0, wa, ba, wx, bx, lam):
    B, T, _ = xc.shape
    xf = xc.astype(jnp.float32)
    xb = xf.reshape(B, T, LRU_BLOCKS, LRU_BLOCK)
    r = jax.nn.sigmoid(jnp.einsum('btni,nij->btnj', xb, wa).reshape(B, T, LRU_WIDTH) + ba)
    i = jax.nn.sigmoid(jnp.einsum('btni,nij->btnj', xb, wx).reshape(B, T, LRU_WIDTH) + bx)
    log_a = -LRU_C * r * jax.nn.softplus(-lam)
    a = jnp.exp(log_a)
    u = jnp.sqrt(-jnp.expm1(2.0 * log_a)) * i * xf
    u = u.at[:, 0].add(a[:, 0] * h0.astype(jnp.float32))

    def comb(left, right):
        return (left[0] * right[0], right[0] * left[1] + right[1])

    _, h = lax.associative_scan(comb, (a, u), axis=1)
    return h, h[:, -1]

def mla_attend(q_nope, q_rope, k_nope, k_rope, v, P):
    T = q_nope.shape[1]
    q_chunk = np.arange(P, P + T) // CHUNK
    k_chunk = np.arange(P + T) // CHUNK
    scale = (MLA_NOPE + MLA_ROPE) ** -0.5
    outs = []
    for s in range(0, T, QBLOCK):
        e = min(s + QBLOCK, T)
        kend = P + min(T, -(-e // CHUNK) * CHUNK)
        sc = (jnp.einsum('bqhd,bkhd->bhqk', q_nope[:, s:e], k_nope[:, :kend])
              + jnp.einsum('bqhd,bkd->bhqk', q_rope[:, s:e], k_rope[:, :kend])) * scale
        mask = jnp.asarray(k_chunk[None, :kend] <= q_chunk[s:e, None])
        sc = jnp.where(mask, sc.astype(jnp.float32), -jnp.inf)
        p = jax.nn.softmax(sc, axis=-1)
        outs.append(jnp.einsum('bhqk,bkhd->bqhd', p, v[:, :kend]))
    return jnp.concatenate(outs, axis=1)

def retention(q, k, v, S0):
    T = q.shape[1]
    L = min(CHUNK, T)
    lg = jnp.log(1.0 - 2.0 ** (-5.0 - jnp.arange(RET_HEADS, dtype=jnp.float32)))
    idx = jnp.arange(L, dtype=jnp.float32)
    diff = idx[:, None] - idx[None, :]
    causal = diff >= 0
    dmat = jnp.where(causal[None], jnp.exp(jnp.where(causal, diff, 0.0)[None] * lg[:, None, None]), 0.0)
    cross = jnp.exp((idx[:, None] + 1.0) * lg[None, :])
    tail = jnp.exp((L - 1.0 - idx)[None, :] * lg[:, None])
    whole = jnp.exp(L * lg)

    def step(S, inp):
        qc, kc, vc = inp
        att = jnp.einsum('bihd,bjhd->bhij', qc, kc) * dmat
        y = (jnp.einsum('bhij,bjhe->bihe', att, vc)
             + jnp.einsum('bihd,bhde->bihe', qc, S) * cross[None, :, :, None])
        S = whole[None, :, None, None] * S + jnp.einsum('bjhd,bjhe,hj->bhde', kc, vc, tail)
        return S, y

    xs = (to_chunks(q.astype(jnp.float32), L), to_chunks(k.astype(jnp.float32), L),
          to_chunks(v.astype(jnp.float32), L))
    S, ys = lax.scan(step, S0.astype(jnp.float32), xs)
    return from_chunks(ys), S

def mlstm(q, k, v, ig, lf, C0, n0, m0):
    T = q.shape[1]
    L = min(CHUNK, T)
    tril = jnp.tril(jnp.ones((L, L), dtype=bool))

    def step(carry, inp):
        C, n, m = carry
        qc, kc, vc, igc, lfc = inp
        bh = jnp.cumsum(lfc, axis=1).transpose(0, 2, 1)
        igh = igc.transpose(0, 2, 1)
        dm = jnp.where(tril, bh[..., :, None] - bh[..., None, :] + igh[..., None, :], -jnp.inf)
        m_state = bh + m[..., None]
        m_t = jnp.maximum(m_state, jnp.max(dm, axis=-1))
        sc = jnp.einsum('bthd,bshd->bhts', qc, kc) * jnp.exp(dm - m_t[..., None])
        g = jnp.exp(m_state - m_t)
        num = jnp.einsum('bhts,bshe->bhte', sc, vc) + g[..., None] * jnp.einsum('bthd,bhed->bhte', qc, C)
        den = jnp.sum(sc, axis=-1) + g * jnp.einsum('bthd,bhd->bht', qc, n)
        hh = num / jnp.maximum(jnp.abs(den), jnp.exp(-m_t))[..., None]
        m_new = m_t[..., -1]
        ws = jnp.exp(bh[..., -1:] - bh + igh - m_new[..., None])
        gl = jnp.exp(bh[..., -1] + m - m_new)
        C = gl[..., None, None] * C + jnp.einsum('bhs,bshe,bshd->bhed', ws, vc, kc)
        n = gl[..., None] * n + jnp.einsum('bhs,bshd->bhd', ws, kc)
        return (C, n, m_new), hh.transpose(0, 2, 1, 3)

    carry0 = (C0.astype(jnp.float32), n0.astype(jnp.float32), m0.astype(jnp.float32))
    xs = tuple(to_chunks(a.astype(jnp.float32), L) for a in (q, k, v, ig, lf))
    (C, n, m), hs = lax.scan(step, carry0, xs)
    return from_chunks(hs), (C, n, m)

def layer(x, past_ckv, past_krope, lru_h, lru_conv, ret_S, m_C, m_n, m_m, lp):
    B, T, _ = x.shape
    P = past_ckv.shape[1]
    pos = jnp.arange(P, P + T, dtype=jnp.float32)
    h = rms(x, lp['norm_mix'])
    proj = h @ lp['w_in']
    (lru_x, lru_g, q_lat, kv_lat, k_rp, r_q, r_k, r_v, r_g,
     m_q, m_k, m_v, m_o, m_if) = jnp.split(proj, np.cumsum(IN_SIZES)[:-1].tolist(), axis=-1)

    xc, conv_new = causal_conv(lru_x, lru_conv, lp['lru_conv_w'], lp['lru_conv_b'])
    y_a, h_new = rglru(xc, lru_h, lp['lru_wa'], lp['lru_ba'], lp['lru_wx'], lp['lru_bx'], lp['lru_lambda'])

    q = (rms(q_lat, lp['mla_q_norm']) @ lp['mla_wq_b']).reshape(B, T, MLA_HEADS, MLA_NOPE + MLA_ROPE)
    q_nope = rms(q[..., :MLA_NOPE], lp['mla_qn_norm'])
    q_rope = rope(rms(q[..., MLA_NOPE:], lp['mla_qr_norm']), pos)
    ckv_new = rms(kv_lat, lp['mla_kv_norm'])
    krope_new = rope(rms(k_rp, lp['mla_kr_norm'])[:, :, None, :], pos)[:, :, 0, :]
    ckv_all = jnp.concatenate([past_ckv.astype(jnp.float32), ckv_new], axis=1)
    kr_all = jnp.concatenate([past_krope.astype(jnp.float32), krope_new], axis=1)
    kv = (ckv_all @ lp['mla_wkv_b']).reshape(B, P + T, MLA_HEADS, MLA_NOPE + MLA_V)
    k_nope = rms(kv[..., :MLA_NOPE], lp['mla_kn_norm'])
    y_b = mla_attend(q_nope, q_rope, k_nope, kr_all, kv[..., MLA_NOPE:], P).reshape(B, T, MLA_HEADS * MLA_V)

    rq = rope(r_q.reshape(B, T, RET_HEADS, RET_DK), pos)
    rk = rope(r_k.reshape(B, T, RET_HEADS, RET_DK), pos) * RET_DK ** -0.5
    y_c, S_new = retention(rq, rk, r_v.reshape(B, T, RET_HEADS, RET_DV), ret_S)

    b_if = lp['mlstm_b_if']
    ig = m_if[..., :MLSTM_HEADS] + b_if[:MLSTM_HEADS]
    lf = jax.nn.log_sigmoid(m_if[..., MLSTM_HEADS:] + b_if[MLSTM_HEADS:])
    y_d, (C_new, n_new, mm_new) = mlstm(
        m_q.reshape(B, T, MLSTM_HEADS, MLSTM_DK),
        m_k.reshape(B, T, MLSTM_HEADS, MLSTM_DK) * MLSTM_DK ** -0.5,
        m_v.reshape(B, T, MLSTM_HEADS, MLSTM_DV), ig, lf, m_C, m_n, m_m)

    on = lp['out_norm']
    G = GROUP_WIDTH
    y_a = head_rms(y_a, on[:G]) * jax.nn.gelu(lru_g)
    y_b = head_rms(y_b, on[G:2 * G])
    y_c = head_rms(y_c.reshape(B, T, -1), on[2 * G:3 * G]) * jax.nn.silu(r_g)
    y_d = head_rms(y_d.reshape(B, T, -1), on[3 * G:]) * jax.nn.sigmoid(m_o)
    x = x + jnp.concatenate([y_a, y_b, y_c, y_d], axis=-1) @ lp['w_out']

    gu = rms(x, lp['norm_ffn']) @ lp['w_gu']
    x = x + (jax.nn.silu(gu[..., :FFN_HIDDEN]) * gu[..., FFN_HIDDEN:]) @ lp['w_down']
    return x, (ckv_new, krope_new, h_new, conv_new, S_new, C_new, n_new, mm_new)

def setup_inputs(seed: int = 0) -> dict:
    key = jax.random.key(seed)
    keys = jax.random.split(key, 48)
    cnt = [0]
    f32 = jnp.float32

    def nxt():
        cnt[0] += 1
        return keys[cnt[0] - 1]

    def nrm(shape, scale):
        return jax.random.normal(nxt(), shape, f32) * scale

    def gain(shape):
        return 1.0 + 0.05 * jax.random.normal(nxt(), shape, f32)

    def unif(shape, lo, hi):
        return jax.random.uniform(nxt(), shape, f32, lo, hi)

    res = 1.0 / math.sqrt(2 * DEPTH)
    inp = {}
    inp['x_prompt'] = nrm((BATCH, SEQ, D_MODEL), 1.0)
    inp['x_sample'] = nrm((DEC_BATCH, DEC_SEQ, D_MODEL), 1.0)
    inp['cache_mla_ckv'] = nrm((DEPTH, DEC_BATCH, PAST_LEN, MLA_KV_RANK), 1.0)
    inp['cache_mla_krope'] = nrm((DEPTH, DEC_BATCH, PAST_LEN, MLA_ROPE), 1.0)
    inp['state_lru_h'] = nrm((DEPTH, DEC_BATCH, LRU_WIDTH), 0.5)
    inp['state_lru_conv'] = nrm((DEPTH, DEC_BATCH, CONV_W - 1, LRU_WIDTH), 1.0)
    inp['state_ret'] = nrm((DEPTH, DEC_BATCH, RET_HEADS, RET_DK, RET_DV), 0.3)
    inp['state_mlstm_C'] = nrm((DEPTH, DEC_BATCH, MLSTM_HEADS, MLSTM_DV, MLSTM_DK), 0.3)
    inp['state_mlstm_n'] = nrm((DEPTH, DEC_BATCH, MLSTM_HEADS, MLSTM_DK), 0.3)
    inp['state_mlstm_m'] = unif((DEPTH, DEC_BATCH, MLSTM_HEADS), 0.0, 2.0)
    inp['norm_mix'] = gain((DEPTH, D_MODEL))
    inp['w_in'] = nrm((DEPTH, D_MODEL, IN_DIM), D_MODEL ** -0.5)
    inp['lru_conv_w'] = nrm((DEPTH, CONV_W, LRU_WIDTH), CONV_W ** -0.5)
    inp['lru_conv_b'] = nrm((DEPTH, LRU_WIDTH), 0.01)
    inp['lru_wa'] = nrm((DEPTH, LRU_BLOCKS, LRU_BLOCK, LRU_BLOCK), LRU_BLOCK ** -0.5)
    inp['lru_ba'] = nrm((DEPTH, LRU_WIDTH), 0.01)
    inp['lru_wx'] = nrm((DEPTH, LRU_BLOCKS, LRU_BLOCK, LRU_BLOCK), LRU_BLOCK ** -0.5)
    inp['lru_bx'] = nrm((DEPTH, LRU_WIDTH), 0.01)
    u = unif((DEPTH, LRU_WIDTH), 0.9, 0.999) ** (1.0 / LRU_C)
    inp['lru_lambda'] = jnp.log(u) - jnp.log1p(-u)
    inp['mla_q_norm'] = gain((DEPTH, MLA_Q_RANK))
    inp['mla_wq_b'] = nrm((DEPTH, MLA_Q_RANK, MLA_HEADS * (MLA_NOPE + MLA_ROPE)), MLA_Q_RANK ** -0.5)
    inp['mla_qn_norm'] = gain((DEPTH, MLA_NOPE))
    inp['mla_qr_norm'] = gain((DEPTH, MLA_ROPE))
    inp['mla_kv_norm'] = gain((DEPTH, MLA_KV_RANK))
    inp['mla_kr_norm'] = gain((DEPTH, MLA_ROPE))
    inp['mla_wkv_b'] = nrm((DEPTH, MLA_KV_RANK, MLA_HEADS * (MLA_NOPE + MLA_V)), MLA_KV_RANK ** -0.5)
    inp['mla_kn_norm'] = gain((DEPTH, MLA_NOPE))
    inp['mlstm_b_if'] = jnp.concatenate([nrm((DEPTH, MLSTM_HEADS), 0.1),
                                         unif((DEPTH, MLSTM_HEADS), 3.0, 6.0)], axis=-1)
    inp['out_norm'] = gain((DEPTH, D_MODEL))
    inp['w_out'] = nrm((DEPTH, D_MODEL, D_MODEL), D_MODEL ** -0.5 * res)
    inp['norm_ffn'] = gain((DEPTH, D_MODEL))
    inp['w_gu'] = nrm((DEPTH, D_MODEL, 2 * FFN_HIDDEN), D_MODEL ** -0.5)
    inp['w_down'] = nrm((DEPTH, FFN_HIDDEN, D_MODEL), FFN_HIDDEN ** -0.5 * res)
    return inp

def reference(x_prompt, x_sample, cache_mla_ckv, cache_mla_krope, state_lru_h, state_lru_conv,
              state_ret, state_mlstm_C, state_mlstm_n, state_mlstm_m,
              norm_mix, w_in, lru_conv_w, lru_conv_b, lru_wa, lru_ba, lru_wx, lru_bx, lru_lambda,
              mla_q_norm, mla_wq_b, mla_qn_norm, mla_qr_norm, mla_kv_norm, mla_kr_norm, mla_wkv_b,
              mla_kn_norm, mlstm_b_if, out_norm, w_out, norm_ffn, w_gu, w_down):
    f32 = jnp.float32
    Bp = x_prompt.shape[0]
    yp = x_prompt
    ys = x_sample
    p_acc = [[] for _ in range(8)]
    s_acc = [[] for _ in range(8)]
    for l in range(DEPTH):
        lp = {'norm_mix': norm_mix[l], 'w_in': w_in[l],
              'lru_conv_w': lru_conv_w[l], 'lru_conv_b': lru_conv_b[l],
              'lru_wa': lru_wa[l], 'lru_ba': lru_ba[l], 'lru_wx': lru_wx[l], 'lru_bx': lru_bx[l],
              'lru_lambda': lru_lambda[l],
              'mla_q_norm': mla_q_norm[l], 'mla_wq_b': mla_wq_b[l], 'mla_qn_norm': mla_qn_norm[l],
              'mla_qr_norm': mla_qr_norm[l], 'mla_kv_norm': mla_kv_norm[l], 'mla_kr_norm': mla_kr_norm[l],
              'mla_wkv_b': mla_wkv_b[l], 'mla_kn_norm': mla_kn_norm[l],
              'mlstm_b_if': mlstm_b_if[l], 'out_norm': out_norm[l], 'w_out': w_out[l],
              'norm_ffn': norm_ffn[l], 'w_gu': w_gu[l], 'w_down': w_down[l]}
        yp, st_p = layer(yp,
                         jnp.zeros((Bp, 0, MLA_KV_RANK), f32), jnp.zeros((Bp, 0, MLA_ROPE), f32),
                         jnp.zeros((Bp, LRU_WIDTH), f32), jnp.zeros((Bp, CONV_W - 1, LRU_WIDTH), f32),
                         jnp.zeros((Bp, RET_HEADS, RET_DK, RET_DV), f32),
                         jnp.zeros((Bp, MLSTM_HEADS, MLSTM_DV, MLSTM_DK), f32),
                         jnp.zeros((Bp, MLSTM_HEADS, MLSTM_DK), f32),
                         jnp.zeros((Bp, MLSTM_HEADS), f32), lp)
        ys, st_s = layer(ys, cache_mla_ckv[l], cache_mla_krope[l], state_lru_h[l], state_lru_conv[l],
                         state_ret[l], state_mlstm_C[l], state_mlstm_n[l], state_mlstm_m[l], lp)
        for acc, s in zip(p_acc, st_p):
            acc.append(s)
        for acc, s in zip(s_acc, st_s):
            acc.append(s)
    p_ckv, p_krope, p_lru_h, p_lru_conv, p_ret, p_mC, p_mn, p_mm = [jnp.stack(a) for a in p_acc]
    s_ckv, s_krope, s_lru_h, s_lru_conv, s_ret, s_mC, s_mn, s_mm = [jnp.stack(a) for a in s_acc]
    return (yp, ys, p_ckv, p_krope, p_lru_h, p_lru_conv, p_ret, p_mC, p_mn, p_mm,
            s_ckv, s_krope, s_lru_h, s_lru_conv, s_ret, s_mC, s_mn, s_mm)


_drawn_inputs = setup_inputs


def setup_inputs(seed=0):
    import zlib

    import numpy as np

    out = dict(_drawn_inputs(seed))
    spreads = {}
    factors = {'lru_ba': 23.822,
     'lru_bx': 8.0,
     'mla_q_norm': 3.439,
     'mla_qn_norm': 3.246,
     'mla_qr_norm': 6.754,
     'mla_kn_norm': 3.964}
    for name, (base, spread) in spreads.items():
        noise = np.random.default_rng([zlib.crc32(name.encode()), seed]).standard_normal(out[name].shape)
        drawn = base * np.exp(spread * noise) if base else spread * noise
        out[name] = jnp.asarray(drawn.astype(out[name].dtype))
    for name, factor in factors.items():
        out[name] = (out[name] * factor).astype(out[name].dtype)
    return out
```

```python
from contextlib import ExitStack

import numpy as np
import concourse.bass as bass
from concourse import mybir

ALU = mybir.AluOpType
ACT = mybir.ActivationFunctionType
AX = mybir.AxisListType
F32 = mybir.dt.float32

P = 128
D = 1024
KT = D // P
SEQ, DEC, PAST = 256, 64, 512
DEPTH = 2
T = SEQ + DEC
TP = 384
NT = TP // P
G = 256
H, HD = 4, 64
ROPE = 32
QR = G
KVR = 128
QD = HD + ROPE
FFN = 2816
FT = FFN // P
CONV = 4
AW = SEQ + DEC + CONV - 1
AS = SEQ + CONV - 1
EPS = 1e-6
LRU_C = 8.0
NEG = -1e30
KTILES = 7
SCALE = float(QD) ** -0.5
LG = [float(np.log(1.0 - 2.0 ** (-5.0 - h))) for h in range(H)]

GELU = 2.0 * float(np.sqrt(2.0 / np.pi))
LN_MIN = 2.0 ** -60
SIG_MIN = -43.0
C_LX, C_LG, C_QL, C_KV, C_RQ = 0, 256, 512, 768, 928
C_RK, C_RV, C_RG = C_RQ + G, C_RQ + 2 * G, C_RQ + 3 * G
C_MQ = C_RQ + 4 * G
C_MK, C_MV, C_MO, C_IF = C_MQ + G, C_MQ + 2 * G, C_MQ + 3 * G, C_MQ + 4 * G

SLOT = KT * 264
SLOTS = 5


def constants():
    parts, at, n = [], {}, 0

    def put(name, a):
        nonlocal n
        full = np.zeros((P, a.shape[1]), np.float32)
        full[:a.shape[0]] = a
        at[name] = (n, a.shape[1])
        parts.append(full)
        n += a.shape[1]

    i = np.arange(P)
    put("ident", np.eye(P))
    put("ones", np.ones((P, P)))
    put("headmean", (i[:, None] // HD == i[None, :] // HD) / HD)
    put("swap", (i[:, None] == (i[None, :] ^ 32)))
    diff = np.full((P, 512), -1, np.int64)
    diff[:, 0:256] = np.arange(256)[None, :] - i[:, None]
    diff[:, 256:384] = np.arange(128)[None, :] - i[:, None]
    diff[:, 448:512] = np.arange(64)[None, :] - i[:, None]
    ok = diff >= 0
    put("negmask", np.where(ok, 0.0, NEG))
    lg = np.log(1.0 - 2.0 ** (-5.0 - np.arange(H)))
    put("decay", np.concatenate([np.where(ok, np.exp(np.where(ok, diff, 0) * lg[h]), 0.0) for h in range(H)], 1))
    row_head = lambda pair: 2 * pair + i // HD
    put("cross", np.concatenate([np.exp((np.arange(DEC)[None, :] + 1.0) * lg[row_head(p)][:, None])
                                 for p in range(2)], 1))
    pos = np.concatenate([np.arange(SEQ), PAST + np.arange(DEC), np.zeros(TP - T)]).astype(np.float32)
    inv = (np.float32(10000.0) ** (-np.arange(32, dtype=np.float32) / np.float32(32))).astype(np.float32)
    ang = (pos[None, :T] * inv[i % 32][:, None]).astype(np.float32)
    put("cos_f", np.cos(ang))
    put("sin_f", np.sin(ang) * np.where(i % 64 < 32, -1.0, 1.0)[:, None])
    inv = (np.float32(10000.0) ** (-np.arange(16, dtype=np.float32) / np.float32(16))).astype(np.float32)
    ang = (pos[:, None] * inv[None, :]).astype(np.float32).reshape(NT, P, 16).transpose(1, 0, 2)
    put("cos_t", np.concatenate([np.cos(ang), np.cos(ang)], 2).reshape(P, NT * 32))
    put("sin_t", np.sin(ang).reshape(P, NT * 16))
    put("headrow", np.repeat(np.eye(H), P, 1))
    put("pairrow", np.concatenate([(row_head(p)[None, :] == np.arange(H)[:, None]) for p in range(2)], 1))
    put("early", (i[None, :] < 64) * (i[:, None] == 0))
    put("late", np.where(i[:, None] == 0, NEG, 0.0) * np.ones((1, 64)))
    return np.concatenate(parts, 1).astype(np.float32), at


NCONST = constants()[0].shape[1]

ROWS = {}
_n = 0
for _name, _k in (("norm_mix", DEPTH * KT), ("norm_ffn", DEPTH * KT), ("out_norm", DEPTH * KT),
                  ("conv_w", DEPTH * CONV * 2), ("conv_b", DEPTH * 2), ("ba", DEPTH * 2), ("bx", DEPTH * 2),
                  ("lam", DEPTH * 2), ("q_norm", DEPTH * 2), ("h0", DEPTH * 2), ("conv0", DEPTH * 3 * 2),
                  ("qn", DEPTH), ("kn", DEPTH), ("b_if", DEPTH)):
    ROWS[_name] = _n
    _n += _k
NROWS = _n

def layer_uses():
    u = [("cpT", (2,)), ("ms1", (3,))]
    dense = [0]

    def d(*names):
        for n in names:
            u.append((n, (dense[0] % 2,)))
            dense[0] += 1

    d("ql0", "ql1", "kvr", "mif", "mo0", "mo1", "mo2", "mv0", "mv1", "mv2")
    u += [("cnT", (4,)), ("qms", (5,)), ("qt0", (6,)), ("qt1", (7,)), ("qt2", (2,)), ("lfr", (3,))]
    d("mq0", "mq1", "mk0", "mk1")
    u += [(f"kv{i}", ((4, 5, 6, 7)[i % 4],)) for i in range(KTILES)]
    u += [("rT", (3,)), ("gx", (2,)), ("mkt", (6, 7))]
    for h in range(H):
        u += [(f"ds{h}", (2 + h % 2,)), (f"dd{h}", (4 + h % 2,)), (f"do{h}", (6 + h % 2,))]
    d("rq0", "rq1", "rk0", "rk1")
    fill = [("rqs0", "rqs1", "rg0"), ("rg1", "rg2"), ("rks0", "rks1", "rv0"),
            ("rv1", "rv2", "rkt0", "rkt1")]
    for h in range(H):
        u += [(f"bk{h}", (4, 5)), (f"bq{h}", (6,)), (f"bs{h}", (2, 3))]
        for n in fill[h]:
            d(n)
        u += [(f"bp{h}", (4, 5)), (f"bo{h}", (7,))]
        if h == 0:
            u += [("dT", (2, 3))]
    u += [("bT", (6, 7))]
    fill = ["lx0", "lx1", "lg0", "lg1"]
    for h in range(H):
        u += [(f"cs{h}", (2 + h % 2,)), (f"co{h}", (4 + h % 2,))]
        d(fill[h])
    u += [("ga0", (6,)), ("gx0_", (7,)), ("ga1", (4,)), ("gx1_", (5,)), ("cT", (4, 5)),
          ("am0", (6,)), ("am1", (7,))]
    u += [(f"o{n}", (n,)) for n in range(KT)]
    u += [("ms2", (0,))]
    for j in range(FT):
        u += [(f"fg{j}", ((0, 2, 5)[j % 3],)), (f"fu{j}", ((1, 3, 6)[j % 3],))]
    u += [(f"y{n}", ((7, 4, 5, 6)[n % 4],)) for n in range(KT)]
    return u


def weight_chunks():
    c = [("ql", "w_in", C_QL, 256), ("kvr", "w_in", C_KV, 160), ("mo", "w_in", C_MO, 264),
         ("mv", "w_in", C_MV, 256), ("mq", "w_in", C_MQ, 256), ("mk", "w_in", C_MK, 256),
         ("rq", "w_in", C_RQ, 256), ("rk", "w_in", C_RK, 256), ("rg", "w_in", C_RG, 256),
         ("rv", "w_in", C_RV, 256), ("lx", "w_in", C_LX, 256), ("lg", "w_in", C_LG, 256)]
    c += [(f"o{i}", "w_out", 256 * i, 256) for i in range(4)]
    c += [(f"f{j}", "w_gu", P * j, P) for j in range(FT)]
    c += [(f"y{q}_{r}", "w_down", 256 * q, r) for q in range(4) for r in range(3)]
    return c


CHUNKS = weight_chunks()
CHUNK_AT = {c[0]: i for i, c in enumerate(CHUNKS)}
NCH = len(CHUNKS)
LAST_USE = {"kvr": "kvr", "ql": "ql1", "mo": "mo2", "mv": "mv2", "mq": "mq1", "mk": "mk1", "rq": "rq1",
            "rk": "rk1", "rg": "rg2", "rv": "rv2", "lx": "lx1", "lg": "lg1"}
LAST_USE.update({f"o{i}": f"o{2 * i + 1}" for i in range(4)})
LAST_USE.update({f"f{j}": f"fu{j}" for j in range(FT)})
LAST_USE.update({f"y{q}_{r}": f"y{2 * q + 1}" for q in range(4) for r in range(3)})


def build(nc, I, O):
    with ExitStack() as ctx:
        def sb(name, shape):
            return ctx.enter_context(nc.sbuf_tensor(name, shape, F32))

        sems = {}

        def sem(name):
            if name not in sems:
                sems[name] = ctx.enter_context(nc.semaphore(name))
            return sems[name]

        ring = sb("ring", [P, SLOTS, SLOT])
        cst = sb("cst", [P, NCONST])
        _, cat = constants()

        def C(name, rows=P):
            a, n = cat[name]
            return cst[0:rows, a:a + n]

        ident = C("ident")
        xT = sb("xT", [P, KT, T])
        hT = sb("hT", [P, KT, TP])
        mixT = sb("mixT", [P, KT, T])
        sq = mixT
        rstd = sb("rstd", [P, T])
        cols = sb("cols", [P, NROWS])
        bcn = sb("bcn", [P, DEPTH, KVR + 2 * ROPE])
        gq = sb("gq", [P, DEPTH])
        c8 = sb("c8", [P, DEPTH * 2])
        c16 = sb("c16", [P, DEPTH * 2])
        lamt = sb("lamt", [P, 4, DEPTH * 2])
        wqb = sb("wqb", [P, 2, H * QD])
        wkvb = sb("wkvb", [P, H * 2 * HD])
        wa = sb("wa", [P, DEPTH, 2, P])
        wx = sb("wx", [P, DEPTH, 2, P])
        pckv = sb("pckv", [P, 4, KVR])
        pkr = sb("pkr", [P, DEPTH, 4, ROPE])
        ct = sb("ct", [P, DEPTH, H, HD + 1])
        csn = sb("csn", [HD + 1, DEPTH, H, HD])
        s0c = sb("s0c", [P, DEPTH, 2, HD])
        s0n = sb("s0n", [HD, DEPTH, H, HD])
        m0 = sb("m0", [H, DEPTH])
        eps_c = sb("eps_c", [P, 1])
        one_c = sb("one_c", [P, 1])

        AR = 10624
        arena = sb("arena", [P, AR])

        def view(base, n, **kw):
            assert base + n <= AR, (base, n)
            return arena[:, base:base + n]

        xtm = view(0, NT * D).rearrange("p (t n) -> p t n", t=NT)
        aT = view(0, FT * T).rearrange("p (j n) -> p j n", j=FT)
        fe = view(FT * T, 3 * T).rearrange("p (j n) -> p j n", j=3)
        fs = view(FT * T + 3 * T, T)
        b = 0
        def take(n):
            nonlocal b
            b += n
            return view(b - n, n)
        ckvT = take(KTILES * P)
        vb = take(KTILES * G).rearrange("p (k h e) -> p k h e", k=KTILES, h=H)
        kb = take(KTILES * H * QD).rearrange("p (k h e) -> p k h e", k=KTILES, h=H)
        qtm = take(NT * H * QD).rearrange("p (t h e) -> p t h e", t=NT, h=H)
        ckvn = take(NT * KVR).rearrange("p (t n) -> p t n", t=NT)
        krn = take(NT * ROPE).rearrange("p (t n) -> p t n", t=NT)
        krr = take(NT * ROPE).rearrange("p (t n) -> p t n", t=NT)
        small = take(192)
        bstart = b
        qlT = view(bstart, 2 * TP).rearrange("p (k n) -> p k n", k=2)
        qls = view(bstart + 2 * TP, 2 * TP).rearrange("p (k n) -> p k n", k=2)
        qsq = view(bstart, NT * H * QD).rearrange("p (t h e) -> p t h e", t=NT, h=H)
        ksq = view(bstart + 1152, G).rearrange("p (h e) -> p h e", h=H)
        kT = view(bstart, KTILES * P)
        qT = view(bstart + 896, TP)
        pr = view(bstart + 1280, 1024)
        pT = view(bstart + 2304, 1024)
        b = 0
        xpad = take(2 * 326).rearrange("p (k n) -> p k n", k=2)
        xc = take(2 * AW).rearrange("p (k n) -> p k n", k=2)
        lg = take(2 * AW).rearrange("p (k n) -> p k n", k=2)
        gg = take(2 * AW).rearrange("p (k n) -> p k n", k=2)
        ri = take(4 * AW).rearrange("p (g k n) -> p g k n", g=2, k=2)
        ay = take(2 * AW).rearrange("p (k n) -> p k n", k=2)
        aa = take(2 * AW).rearrange("p (k n) -> p k n", k=2)
        aw = take(2 * AW).rearrange("p (k n) -> p k n", k=2)
        an = take(2 * AW).rearrange("p (k n) -> p k n", k=2)
        ln3 = take(6 * AW).rearrange("p (g n) -> p g n", g=3)
        ah = take(2 * AW).rearrange("p (k n) -> p k n", k=2)

        qh = sb("qh", [P, H, T])
        kf = sb("kf", [P, 2, TP])
        raw = sb("raw", [P, 4, T])
        raws = [raw[:, n, :] for n in range(4)]
        ktm = sb("ktm", [P, NT, G])
        vaug = sb("vaug", [P, NT, H, HD + 1])
        gate = sb("gate", [P, NT, G])
        dmx = sb("dmx", [P, 512])
        dh = sb("dh", [P, 2, 512])
        wt = sb("wt", [P, 2, 576])
        vw = sb("vw", [P, 2, NT, HD + 1])
        qg = sb("qg", [P, H, P])
        ytm = sb("ytm", [P, NT, H, HD])
        ybm = sb("ybm", [P, NT, H, HD])
        dhf = dh[:, :, :].rearrange("p a n -> p (a n)")
        ysq = dhf[:, 0:NT * G].rearrange("p (t h e) -> p t h e", t=NT, h=H)
        rows = gate[0:NROWS, 0, 0:P]
        cin = dhf[:, 0:DEPTH * 256].rearrange("p (l k a d) -> p l k a d", l=DEPTH, k=2, a=2)
        yst = sb("yst", [P, 6, NT * H])
        sst = sb("sst", [HD + 1, 2, 2, HD])
        gif = raw[0:8, 0, :]
        gl8 = raw[0:8, 1:2, :]
        lfr = raw[0:H, 2, :]
        bro = raw[0:H, 3, :]
        mro = sb("mro", [H, T])
        r1 = sb("r1", [H, TP])
        r2 = sb("r2", [H, T])
        r3 = sb("r3", [H, DEC])
        nm = sb("nm", [H, TP])
        ctm = sb("ctm", [P, NT, H])
        em = sb("em", [P, NT, H])
        glb = sb("glb", [P, H + 2 * DEC])

        ps = ctx.enter_context(nc.psum_tensor("ps", [P, 8, 512], F32))
        flat = ps[:, :, :].rearrange("p b n -> p (b n)")

        def col(name, i, rows_=P):
            return cols[0:rows_, ROWS[name] + i:ROWS[name] + i + 1]

        uses = layer_uses()
        banks = dict(uses)
        nfill = [sum(u[1][0] == k for u in uses) for k in range(8)]
        order = {}
        seen = [0] * 8
        for n, bk in uses:
            seen[bk[0]] += 1
            order[n] = seen[bk[0]]
        before = {}
        last = [None] * 8
        for n, bk in uses:
            before[n] = [last[k] for k in bk]
            for k in bk:
                last[k] = n
        filled = [sem(f"filled{k}") for k in range(8)]
        read = [sem(f"read{k}") for k in range(8)]

        def wait_filled(eng, use, l):
            k = banks[use][0]
            eng.wait_ge(filled[k], l * nfill[k] + order[use])

        def claim(pe, use, l):
            for prev in before[use]:
                if prev is not None:
                    k = banks[prev][0]
                    pe.wait_ge(read[k], l * nfill[k] + order[prev])
                elif l > 0:
                    for k in {banks[last[b_]][0] for b_ in banks[use]}:
                        pe.wait_ge(read[k], l * nfill[k])
                else:
                    pe.wait_ge(sem("x_turned"), KT)
                    pe.wait_ge(sem("cols_ready"), 1)
                    pe.wait_ge(sem("ct_ready"), 1)

        def bank(use, a, n, rows_=P):
            base = banks[use][0] * 512
            return flat[0:rows_, base + a:base + a + n]

        made = {}
        per = {}

        def need(eng, name, l, n, k=None):
            assert per.setdefault(name, n) == n, name
            eng.wait_ge(sem(name), l * n + (n if k is None else k))

        def stepper(eng, chain):
            def step(ins, name=None, bank_read=None):
                if bank_read is not None:
                    use, l = bank_read
                    k = banks[use][0]
                    ins.then_inc(read[k], 1)
                    eng.wait_ge(read[k], l * nfill[k] + order[use])
                    return
                k = name or chain
                made[k] = made.get(k, 0) + 1
                ins.then_inc(sem(k), 1)
                eng.wait_ge(sem(k), made[k])
            return step

        def now_read(eng, use):
            eng.sem_inc(read[banks[use][0]], 1)

        def now_made(eng, name):
            made[name] = made.get(name, 0) + 1
            eng.sem_inc(sem(name), 1)

        def wait_bank_read(eng, use, l):
            k = banks[use][0]
            eng.wait_ge(read[k], l * nfill[k] + order[use])

        block = ctx.enter_context(nc.Block())

        SMALL = []
        r = ROWS

        def row(name, n, src):
            SMALL.append((rows[r[name]:r[name] + n, 0:src.shape[-1]], src))

        row("norm_mix", DEPTH * KT, I["norm_mix"].rearrange("l (k p) -> (l k) p", p=P))
        row("norm_ffn", DEPTH * KT, I["norm_ffn"].rearrange("l (k p) -> (l k) p", p=P))
        row("out_norm", DEPTH * KT, I["out_norm"].rearrange("l (k p) -> (l k) p", p=P))
        row("conv_w", DEPTH * CONV * 2, I["lru_conv_w"].rearrange("l j (k p) -> (l j k) p", p=P))
        row("conv_b", DEPTH * 2, I["lru_conv_b"].rearrange("l (k p) -> (l k) p", p=P))
        row("ba", DEPTH * 2, I["lru_ba"].rearrange("l (k p) -> (l k) p", p=P))
        row("bx", DEPTH * 2, I["lru_bx"].rearrange("l (k p) -> (l k) p", p=P))
        row("lam", DEPTH * 2, I["lru_lambda"].rearrange("l (k p) -> (l k) p", p=P))
        row("q_norm", DEPTH * 2, I["mla_q_norm"].rearrange("l (k p) -> (l k) p", p=P))
        row("h0", DEPTH * 2, I["state_lru_h"].rearrange("l b (k p) -> (l b k) p", p=P))
        row("conv0", DEPTH * 6, I["state_lru_conv"].rearrange("l b j (k p) -> (l b j k) p", p=P))
        row("qn", DEPTH, I["mla_qn_norm"])
        row("kn", DEPTH, I["mla_kn_norm"])
        row("b_if", DEPTH, I["mlstm_b_if"])
        NROWLOADS = len(SMALL)
        SMALL.append((bcn[:, :, 0:KVR], I["mla_kv_norm"].partition_broadcast(P)))
        SMALL.append((bcn[:, :, KVR:KVR + ROPE], I["mla_kr_norm"].partition_broadcast(P)))
        SMALL.append((bcn[:, :, KVR + ROPE:], I["mla_qr_norm"].partition_broadcast(P)))
        SMALL.append((m0[:, :], I["state_mlstm_m"].rearrange("l b h -> (b h) l")))
        for l in range(DEPTH):
            SMALL.append((pkr[:, l], I["cache_mla_krope"][l, 0].rearrange("(a p) c -> p a c", p=P)))
            SMALL.append((csn[0:HD, l], I["state_mlstm_C"][l, 0].rearrange("h e d -> e h d")))
            SMALL.append((csn[HD:HD + 1, l], I["state_mlstm_n"][l]))
            SMALL.append((s0n[:, l], I["state_ret"][l, 0].rearrange("h d e -> d h e")))
            s0v = I["state_ret"][l, 0].rearrange("(p a) d e -> a d p e", a=2)
            cv = I["state_mlstm_C"][l, 0].rearrange("(p a) e d -> a e p d", a=2)
            nv = I["state_mlstm_n"][l, 0].rearrange("(p a) d -> a d p", a=2)
            wav = I["lru_wa"][l].rearrange("(t a) i j -> a i t j", a=2)
            wxv = I["lru_wx"][l].rearrange("(t a) i j -> a i t j", a=2)
            for a in range(2):
                rs = slice(a * HD, (a + 1) * HD)
                SMALL.append((s0c[rs, l], s0v[a]))
                SMALL.append((cin[rs, l, :, a, :], cv[a]))
                SMALL.append((ct[rs, l, a::2, HD], nv[a]))
                SMALL.append((wa[rs, l, :, rs], wav[a]))
                SMALL.append((wx[rs, l, :, rs], wxv[a]))
        NSMALL = len(SMALL)

        @block.sync
        def _(sp):
            sp.wait_ge(sem("cleared_small"), 5)
            for dst, src in SMALL[1::2]:
                sp.dma_start(dst, src, allow_slow_non_contiguous=True).then_inc(sem("small_loaded"), 16)
            for l in range(DEPTH):
                w_in = I["w_in"][l].rearrange("(k p) n -> p k n", p=P)
                w_out = I["w_out"][l].rearrange("(k p) n -> p k n", p=P)
                w_gu = I["w_gu"][l].rearrange("(k p) (g n) -> p k g n", p=P, g=2)
                w_dn = I["w_down"][l].rearrange("(k p) n -> p k n", p=P)
                for i, (name, which, c0, n) in enumerate(CHUNKS):
                    g = l * NCH + i
                    if g >= SLOTS:
                        old = g - SLOTS
                        wait_filled(sp, LAST_USE[CHUNKS[old % NCH][0]], old // NCH)
                    slot = ring[:, g % SLOTS, :]
                    loaded = sem(f"loaded{g % SLOTS}")
                    if which == "w_gu":
                        dst = slot[:, 0:KT * 256].rearrange("p (k g n) -> p k g n", k=KT, g=2)
                        for q in range(2):
                            sp.dma_start(dst[:, :, q, :], w_gu[:, :, q, c0:c0 + P]).then_inc(loaded, 16)
                    elif which == "w_down":
                        k0, k1 = 8 * n, min(8 * n + 8, FT)
                        dst = slot[:, 0:(k1 - k0) * 256].rearrange("p (k n) -> p k n", n=256)
                        hf = (k1 - k0) // 2
                        sp.dma_start(dst[:, 0:hf, :], w_dn[:, k0:k0 + hf, c0:c0 + 256]).then_inc(loaded, 16)
                        sp.dma_start(dst[:, hf:, :], w_dn[:, k0 + hf:k1, c0:c0 + 256]).then_inc(loaded, 16)
                    else:
                        src = w_in if which == "w_in" else w_out
                        dst = slot[:, 0:KT * n].rearrange("p (k n) -> p k n", k=KT)
                        for q in range(2):
                            sp.dma_start(dst[:, 4 * q:4 * q + 4, :],
                                         src[:, 4 * q:4 * q + 4, c0:c0 + n]).then_inc(loaded, 16)

        def chunk(name, l, n):
            g = l * NCH + CHUNK_AT[name]
            return ring[:, g % SLOTS, 0:(SLOT // n if n == 264 else KT) * n].rearrange("p (k n) -> p k n", n=n)

        def wait_chunk(eng, name, l):
            g = l * NCH + CHUNK_AT[name]
            eng.wait_ge(sem(f"loaded{g % SLOTS}"), 32 * (g // SLOTS + 1))

        @block.gpsimd
        def _(pool):
            for n, t in enumerate((rows[:, :], cin[:, :, :, :, :], ct[:, :, :, :], wa[:, :, :, :], wx[:, :, :, :])):
                nc.gpsimd.memset(t, 0.0).then_inc(sem("cleared_small"), 1)
            nout = [0]

            def out(dst, src):
                nout[0] += 1
                pool.dma_start(dst, src, allow_slow_non_contiguous=True).then_inc(sem("out_done"), 16)

            def out_wait(mark):
                pool.wait_ge(sem("out_done"), 16 * mark)

            for l in range(DEPTH):
                if l > 0:
                    wait_filled(pool, "kv6", l - 1)
                pool.dma_start(pckv[:, :, :], I["cache_mla_ckv"][l, 0].rearrange("(a p) c -> p a c", p=P)).then_inc(
                    sem("latents_loaded"), 16)
                pool.dma_start(wqb[:, :, :], I["mla_wq_b"][l].rearrange("(k p) n -> p k n", p=P)).then_inc(
                    sem("latents_loaded"), 16)
                pool.dma_start(wkvb[:, :], I["mla_wkv_b"][l]).then_inc(sem("latents_loaded"), 16)
                need(pool, "ckv_new", l, 1)
                out(O["p_ckv"][l, 0].rearrange("(t p) c -> p t c", p=P), ckvn[:, 0:2, :])
                out(O["s_ckv"][l, 0], ckvn[0:DEC, 2, :])
                need(pool, "krope_new", l, 1)
                out(O["p_krope"][l, 0].rearrange("(t p) c -> p t c", p=P), krr[:, 0:2, :])
                out(O["s_krope"][l, 0], krr[0:DEC, 2, :])
                need(pool, "m_rows", l, 1)
                out(O["p_mm"][l].rearrange("b h -> h b"), mro[:, SEQ - 1:SEQ])
                out(O["s_mm"][l].rearrange("b h -> h b"), mro[:, T - 1:T])
                pool.wait_ge(sem("out_done"), 16 * nout[0])
                now_made(pool, "b_out")
                for grp in "dc":
                    for h in range(H):
                        need(pool, f"state_{grp}", l, H, h + 1)
                        for s, pre in ((0, "p"), (1, "s")):
                            if grp == "d":
                                out(O[pre + "_mC"][l, 0, h], sst[0:HD, h % 2, s, :])
                                out(O[pre + "_mn"][l, :, h, :], sst[HD:HD + 1, h % 2, s, :])
                            else:
                                out(O[pre + "_ret"][l, 0, h], sst[0:HD, h % 2, s, :])
                        pool.wait_ge(sem("out_done"), 16 * nout[0])
                        now_made(pool, "state_out")
                need(pool, "lru_x_in", l, 1)
                for s, (pre, e) in enumerate((("p", SEQ), ("s", 323))):
                    for k in range(2):
                        out(O[pre + "_lru_conv"][l, 0, :, k * P:(k + 1) * P].rearrange("j p -> p j"),
                            xpad[:, k, e:e + 3])
                need(pool, "lru_scanned", l, 1)
                for s, (pre, e) in enumerate((("p", SEQ - 1), ("s", AW - 1))):
                    for k in range(2):
                        out(O[pre + "_lru_h"][l, :, k * P:(k + 1) * P].rearrange("b p -> p b"),
                            ah[:, k, e:e + 1])
                pool.wait_ge(sem("out_done"), 16 * nout[0])
                now_made(pool, "a_out")
            for t in range(NT):
                pool.wait_ge(sem("y_out"), 2 * (t + 1))
                if t < 2:
                    out(O["yp"][0, t * P:(t + 1) * P, :], xtm[:, t, :])
                else:
                    out(O["ys"][0], xtm[0:DEC, 2, :])
            pool.wait_ge(sem("out_done"), 16 * nout[0])

        @block.tensor
        def _(pe):
            mm = nc.tensor.matmul

            def fill(ins, use):
                ins.then_inc(filled[banks[use][0]], 1)

            pe.wait_ge(sem("ident_loaded"), 16)
            pe.wait_ge(sem("x_loaded"), 32)
            pe.wait_ge(sem("x_cleared"), 1)
            for k in range(KT):
                for t in range(NT):
                    ins = nc.tensor.transpose(ps[:, k, t * P:(t + 1) * P], xtm[:, t, k * P:(k + 1) * P], ident)
                ins.then_inc(sem("pre_filled"), 1)
            pe.wait_ge(sem("small_loaded"), 16 * NSMALL)
            pe.wait_ge(sem("x_turned"), 1)
            nc.tensor.transpose(ps[:, 0, 0:NROWS], rows[:, :], ident[0:NROWS, 0:NROWS]).then_inc(sem("pre_filled"), 1)
            pe.wait_ge(sem("x_turned"), 2)
            for l in range(DEPTH):
                for p in range(2):
                    ins = nc.tensor.transpose(ps[:, 1, (2 * l + p) * P:(2 * l + p + 1) * P],
                                              cin[:, l, p].rearrange("q a d -> q (a d)"), ident)
            ins.then_inc(sem("pre_filled"), 1)
            pe.wait_ge(sem("consts_loaded"), 16)

            def norm_sum(use, l, which):
                claim(pe, use, l)
                for k in range(KT):
                    need(pe, "squared", l, 2 * KT, which * KT + k + 1)
                    ins = mm(bank(use, 0, T), C("ones"), sq[:, k, :], start=(k == 0), stop=(k == KT - 1))
                fill(ins, use)

            def feature(use, l, name, c, m, cn=256, which=0, wait_h=False):
                claim(pe, use, l)
                wait_chunk(pe, name, l)
                w = chunk(name, l, cn)
                for k in range(KT):
                    if wait_h:
                        need(pe, "normed", l, 2 * KT, which * KT + k + 1)
                    ins = mm(bank(use, 0, T, m), w[:, k, c:c + m], hT[:, k, 0:T], start=(k == 0), stop=(k == KT - 1))
                fill(ins, use)

            def tokens(use, l, name, c, n, t, cn=256):
                claim(pe, use, l)
                wait_chunk(pe, name, l)
                w = chunk(name, l, cn)
                for k in range(KT):
                    ins = mm(bank(use, 0, n), hT[:, k, t * P:(t + 1) * P], w[:, k, c:c + n],
                             start=(k == 0), stop=(k == KT - 1))
                fill(ins, use)

            def key_tiles(use, l, ready, n):
                claim(pe, use, l)
                need(pe, ready, l, n)
                for t in range(NT):
                    for p in range(2):
                        ins = nc.tensor.transpose(bank(use, t * G + p * P, P), kf[:, p, t * P:(t + 1) * P], ident)
                fill(ins, use)

            def causal_scores(use, l, h):
                claim(pe, use, l)
                q, k = qh[:, h, :], kf[:, h // 2, :]
                mm(bank(use, 0, 256), k[:, 0:128], q[:, 0:256], start=True, stop=True)
                mm(bank(use, 256, 192), k[:, 128:256], q[:, 128:320], start=True, stop=True)
                fill(mm(bank(use, 448, 64), k[:, 256:384], q[:, 256:320], start=True, stop=True), use)

            def head_out(use, l, h, wready, e, state, cross, mlstm):
                claim(pe, use, l)
                need(pe, wready, l, H, h + 1)
                w = wt[:, h % 2, :]
                o = lambda t: bank(use, t * e, e)
                mm(o(0), w[:, 0:128], vaug[:, 0, h, 0:e], start=True, stop=True)
                mm(o(1), w[:, 128:256], vaug[:, 0, h, 0:e], start=True, stop=False)
                mm(o(1), w[:, 256:384], vaug[:, 1, h, 0:e], start=False, stop=True)
                mm(o(2), w[:, 448:576], vaug[:, 2, h, 0:e], start=True, stop=False)
                mm(o(2), cross, state, start=False, stop=True)
                for s, tiles in enumerate(((0, 1), (2,))):
                    for t in tiles:
                        a, b_ = vw[:, h % 2, t, 0:e], ktm[:, t, h * HD:(h + 1) * HD]
                        if not mlstm:
                            a, b_ = b_, a
                        ins = mm(bank(use, 200 + 64 * s, 64, e), a, b_, start=(t == tiles[0]), stop=(t == tiles[-1]))
                fill(ins, use)

            def turn_out(use, l, src, ready):
                claim(pe, use, l)
                need(pe, ready, l, 1)
                for p in range(2):
                    for t in range(NT):
                        ins = nc.tensor.transpose(
                            bank(use, p * 512 + t * P, P),
                            src[:, t, 2 * p:2 * p + 2, :].rearrange("q a e -> q (a e)"), ident)
                fill(ins, use)

            for l in range(DEPTH):
                claim(pe, "cpT", l)
                pe.wait_ge(sem("latents_loaded"), 48 * (l + 1))
                for a in range(4):
                    ins = nc.tensor.transpose(bank("cpT", a * P, P), pckv[:, a, :], ident)
                fill(ins, "cpT")
                norm_sum("ms1", l, 0)
                for p in range(2):
                    feature(f"ql{p}", l, "ql", p * P, P, wait_h=(p == 0))
                claim(pe, "kvr", l)
                wait_chunk(pe, "kvr", l)
                w = chunk("kvr", l, 160)
                for t in range(NT):
                    for k in range(KT):
                        ins = mm(bank("kvr", t * 160, 160), hT[:, k, t * P:(t + 1) * P], w[:, k, :],
                                 start=(k == 0), stop=(k == KT - 1))
                fill(ins, "kvr")
                feature("mif", l, "mo", 256, 8, 264)
                for t in range(NT):
                    tokens(f"mo{t}", l, "mo", 0, G, t, 264)
                for t in range(NT):
                    tokens(f"mv{t}", l, "mv", 0, G, t)
                claim(pe, "cnT", l)
                need(pe, "ckv_new", l, 1)
                for t in range(NT):
                    ins = nc.tensor.transpose(bank("cnT", t * P, P), ckvn[:, t, :], ident)
                fill(ins, "cnT")
                claim(pe, "qms", l)
                need(pe, "qlat_sq", l, 2)
                need(pe, "qlat", l, 2)
                for t in range(NT):
                    for p in range(2):
                        ins = mm(bank("qms", t, 1), qls[:, p, t * P:(t + 1) * P], C("ones")[:, 0:1],
                                 start=(p == 0), stop=(p == 1))
                fill(ins, "qms")
                for t in range(NT):
                    claim(pe, f"qt{t}", l)
                    for p in range(2):
                        ins = mm(bank(f"qt{t}", 0, H * QD), qlT[:, p, t * P:(t + 1) * P], wqb[:, p, :],
                                 start=(p == 0), stop=(p == 1))
                    fill(ins, f"qt{t}")
                claim(pe, "lfr", l)
                need(pe, "log_forget", l, 1)
                fill(mm(bank("lfr", 0, T, H), ident[0:8, 4:8], gl8[:, 0, :], start=True, stop=True), "lfr")
                for p in range(2):
                    feature(f"mq{p}", l, "mq", p * P, P)
                for p in range(2):
                    feature(f"mk{p}", l, "mk", p * P, P)
                need(pe, "ckvT", l, 1)
                for i in range(KTILES):
                    claim(pe, f"kv{i}", l)
                    fill(mm(bank(f"kv{i}", 0, 512), ckvT[:, i * P:(i + 1) * P], wkvb[:, :],
                            start=True, stop=True), f"kv{i}")
                claim(pe, "rT", l)
                need(pe, "m_rows", l, 1)
                for n, src in enumerate((r1, nm)):
                    for t in range(NT):
                        ins = nc.tensor.transpose(bank("rT", (n * NT + t) * H, H), src[:, t * P:(t + 1) * P],
                                                  ident[0:H, 0:H])
                fill(ins, "rT")
                claim(pe, "gx", l)
                for h in range(H):
                    mm(bank("gx", h, 1), C("headrow", H)[:, h * P:(h + 1) * P], r3[:, DEC - 1:DEC], start=True, stop=True)
                for p in range(2):
                    ins = mm(bank("gx", H + p * DEC, DEC), C("pairrow", H)[:, p * P:(p + 1) * P], r3[:, :],
                             start=True, stop=True)
                fill(ins, "gx")
                feature("rq0", l, "rq", 0, P)
                key_tiles("mkt", l, "mk_ready", 2)
                need(pe, "mq_ready", l, 2)

                def d_scores(h):
                    causal_scores(f"ds{h}", l, h)
                    u = f"dd{h}"
                    claim(pe, u, l)
                    sel = C("headrow", H)[:, h * P:(h + 1) * P]
                    mm(bank(u, 0, 256), sel, r2[:, 0:256], start=True, stop=True)
                    mm(bank(u, 256, 192), sel, r2[:, 128:320], start=True, stop=True)
                    fill(mm(bank(u, 448, 64), sel, r2[:, 256:320], start=True, stop=True), u)

                d_scores(0)
                for h in range(H):
                    if h + 1 < H:
                        d_scores(h + 1)
                        u, name, p = (("rq1", "rq", 1), ("rk0", "rk", 0), ("rk1", "rk", 1))[h]
                        feature(u, l, name, p * P, P)
                    if h == 0:
                        need(pe, "ktm_d", l, 1)
                        need(pe, "vaug_d", l, 3)
                        need(pe, "qg_d", l, 1)
                    head_out(f"do{h}", l, h, "w_d", HD + 1, ct[:, l, h, :], qg[:, h, :], True)
                need(pe, "kb_ready", l, 1)
                need(pe, "q_ready", l, 1)
                need(pe, "vb_ready", l, KTILES)

                def swap_halves(which, n0):
                    for n in (n0, n0 + 1):
                        u = f"{which}{n - n0}"
                        claim(pe, u, l)
                        need(pe, "raw_c", l, 4, n + 1)
                        fill(mm(bank(u, 0, T), C("swap"), raws[n], start=True, stop=True), u)

                def between(h):
                    if h == 0:
                        tokens("rg0", l, "rg", 0, G, 0)
                    elif h == 1:
                        for t in range(1, NT):
                            tokens(f"rg{t}", l, "rg", 0, G, t)
                    elif h == 2:
                        swap_halves("rks", 2)
                        tokens("rv0", l, "rv", 0, G, 0)
                    else:
                        for t in range(1, NT):
                            tokens(f"rv{t}", l, "rv", 0, G, t)
                        need(pe, "rk_ready", l, 2)
                        for u, tiles in (("rkt0", (0, 1)), ("rkt1", (2,))):
                            claim(pe, u, l)
                            for t in tiles:
                                for p in range(2):
                                    ins = nc.tensor.transpose(bank(u, (t - tiles[0]) * G + p * P, P),
                                                              kf[:, p, t * P:(t + 1) * P], ident)
                            fill(ins, u)

                for h in range(H):
                    u = f"bk{h}"
                    claim(pe, u, l)
                    for i in range(KTILES):
                        ins = nc.tensor.transpose(bank(u, i * P, P, QD), kb[:, i, h, :], ident)
                    fill(ins, u)
                    u = f"bq{h}"
                    claim(pe, u, l)
                    for t in range(NT):
                        ins = nc.tensor.transpose(bank(u, t * P, P, QD), qtm[:, t, h, :], ident)
                    fill(ins, u)
                    if h == 0:
                        swap_halves("rqs", 0)
                    u = f"bs{h}"
                    claim(pe, u, l)
                    need(pe, "kT", l, H, h + 1)
                    need(pe, "qT", l, H, h + 1)
                    k, q = kT[0:QD], qT[0:QD]
                    mm(bank(u, 0, 128), q[:, 0:128], k[:, 0:128], start=True, stop=False)
                    mm(bank(u, 64, 64), C("early"), C("late"), start=False, stop=True)
                    mm(bank(u, 128, 256), q[:, 128:256], k[:, 0:256], start=True, stop=False)
                    mm(bank(u, 320, 64), C("early"), C("late"), start=False, stop=True)
                    mm(bank(u, 448, 64), q[:, 256:384], k[:, 256:320], start=True, stop=True)
                    fill(mm(bank(u, 512, 512), q[:, 256:384], k[:, 384:896], start=True, stop=True), u)
                    between(h)
                    u = f"bp{h}"
                    claim(pe, u, l)
                    need(pe, "probs", l, H, h + 1)
                    for a, w_, rr in ((0, 128, 128), (128, 128, 128), (256, 128, 128), (448, 64, 64),
                                      (512, 128, 128), (640, 128, 128), (768, 128, 128), (896, 128, 128)):
                        dst = bank(u, 384 if a == 448 else a, 128, rr)
                        ins = nc.tensor.transpose(dst, pr[:, a:a + w_], ident)
                    fill(ins, u)
                    u = f"bo{h}"
                    claim(pe, u, l)
                    need(pe, "pT", l, H, h + 1)
                    mm(bank(u, 0, 64), pT[:, 0:128], vb[:, 0, h, :], start=True, stop=True)
                    mm(bank(u, 64, 64), pT[:, 128:256], vb[:, 0, h, :], start=True, stop=False)
                    mm(bank(u, 64, 64), pT[:, 256:384], vb[:, 1, h, :], start=False, stop=True)
                    for i in range(4):
                        mm(bank(u, 128, 64), pT[:, 512 + i * P:512 + (i + 1) * P], vb[:, 3 + i, h, :],
                           start=(i == 0), stop=False)
                    fill(mm(bank(u, 128, 64), pT[0:64, 384:512], vb[0:64, 2, h, :], start=False, stop=True), u)
                    if h == 0:
                        turn_out("dT", l, ytm, "y_d")
                need(pe, "rq_ready", l, 2)
                need(pe, "ktm_c", l, 2)
                need(pe, "vaug_c", l, 3)
                need(pe, "qg_c", l, 1)
                causal_scores("cs0", l, 0)
                for h in range(H):
                    if h + 1 < H:
                        causal_scores(f"cs{h + 1}", l, h + 1)
                    if h == 0:
                        turn_out("bT", l, ybm, "y_b")
                    feature(("lx0", "lx1", "lg0", "lg1")[h], l, ("lx", "lx", "lg", "lg")[h], (h % 2) * P, P)
                    head_out(f"co{h}", l, h, "w_c", HD, s0c[:, l, h // 2, :], qg[:, h, :], False)
                def project(n, ks):
                    u = f"o{n}"
                    wait_chunk(pe, f"o{n // 2}", l)
                    w = chunk(f"o{n // 2}", l, 256)
                    for k in ks:
                        need(pe, f"mix{k // 2}", l, 1)
                        ins = mm(bank(u, 0, T), w[:, k, (n % 2) * P:(n % 2 + 1) * P], mixT[:, k, :],
                                 start=(k == 6), stop=(k == 1), skip_group_check=True)
                    if ks[-1] == 1:
                        fill(ins, u)

                for n in range(2):
                    claim(pe, f"o{n}", l)
                    project(n, (6, 7, 2, 3))
                need(pe, "conv_done", l, 1)
                for t in range(2):
                    for u, w in ((f"ga{t}", wa), (f"gx{t}_", wx)):
                        claim(pe, u, l)
                        fill(mm(bank(u, 0, AW), w[:, l, t, :], xc[:, t, :], start=True, stop=True), u)
                for n in range(2, 4):
                    claim(pe, f"o{n}", l)
                    project(n, (6, 7, 2, 3))
                turn_out("cT", l, ytm, "y_c")
                for n in range(4):
                    project(n, (4, 5))
                for n in range(4, 6):
                    claim(pe, f"o{n}", l)
                    project(n, (6, 7, 2, 3, 4, 5))
                need(pe, "h_sq", l, 1)
                for t in range(2):
                    claim(pe, f"am{t}", l)
                    fill(mm(bank(f"am{t}", 0, AW), C("headmean"), an[:, t, :], start=True, stop=True), f"am{t}")
                claim(pe, "o6", l)
                project(6, (6, 7, 2, 3, 4, 5))
                for n in range(7):
                    project(n, (0, 1))
                claim(pe, "o7", l)
                project(7, (6, 7, 2, 3, 4, 5, 0, 1))
                norm_sum("ms2", l, 1)
                for j in range(FT):
                    for q, u in enumerate((f"fg{j}", f"fu{j}")):
                        claim(pe, u, l)
                        wait_chunk(pe, f"f{j}", l)
                        w = chunk(f"f{j}", l, 256)
                        for k in range(KT):
                            if j == 0 and q == 0:
                                need(pe, "normed", l, 2 * KT, KT + k + 1)
                            ins = mm(bank(u, 0, T), w[:, k, q * P:(q + 1) * P], hT[:, k, 0:T],
                                     start=(k == 0), stop=(k == KT - 1))
                        fill(ins, u)
                for q in range(4):
                    us = (f"y{2 * q}", f"y{2 * q + 1}")
                    for u in us:
                        claim(pe, u, l)
                    for k in range(FT):
                        if k % 8 == 0:
                            wait_chunk(pe, f"y{q}_{k // 8}", l)
                        if q == 0:
                            need(pe, "hidden", l, FT, k + 1)
                        w = chunk(f"y{q}_{k // 8}", l, 256)
                        for s, u in enumerate(us):
                            ins = mm(bank(u, 0, T), w[:, k % 8, s * P:(s + 1) * P], aT[:, k, :],
                                     start=(k == 0), stop=(k == FT - 1), skip_group_check=True)
                            if k == FT - 1:
                                fill(ins, u)
            for t in range(NT):
                w = P if t < 2 else DEC
                for hf in range(2):
                    b_ = 2 * t + hf
                    for k in {banks[last[b_]][0]}:
                        pe.wait_ge(read[k], DEPTH * nfill[k])
                    for k in range(4 * hf, 4 * hf + 4):
                        need(pe, "x_new", DEPTH - 1, 2 * KT)
                        ins = nc.tensor.transpose(ps[0:w, b_, (k % 4) * P:(k % 4 + 1) * P],
                                                  xT[:, k, t * P:t * P + w], ident)
                    ins.then_inc(sem("y_turned"), 1)

        @block.scalar
        def _(act):
            step = stepper(act, "act_chain")
            A = nc.scalar.activation
            act.dma_start(ident, I["consts"][:, 0:P]).then_inc(sem("ident_loaded"), 16)
            act.dma_start(xtm[:, 0:2, :], I["x_prompt"][0].rearrange("(t p) n -> p t n", p=P)).then_inc(sem("x_loaded"), 16)
            act.dma_start(xtm[0:DEC, 2, :], I["x_sample"][0]).then_inc(sem("x_loaded"), 16)
            act.wait_ge(sem("cleared_small"), 5)
            for dst, src in SMALL[0::2]:
                act.dma_start(dst, src, allow_slow_non_contiguous=True).then_inc(sem("small_loaded"), 16)
            act.dma_start(cst[:, P:], I["consts"][:, P:]).then_inc(sem("consts_loaded"), 16)
            act.preload_act_table_set("natural_log_exp_and_others")
            act.wait_ge(sem("eps_set"), 2)
            act.wait_ge(sem("lam_abs"), 1)
            A(lamt[:, 1, :], lamt[:, 0, :], ACT.Exp, scale=-1.0).then_inc(sem("lam_exp"), 1)

            def rsqrt_(l, dst, src, n, rows_=P, name=None, use=None, tmp=None):
                tmp = dst if tmp is None else tmp
                step(A(tmp, src, ACT.Ln, scale=1.0 / n, bias=eps_c[0:rows_, :]), bank_read=(use, l) if use else None)
                step(A(dst, tmp, ACT.Exp, scale=-0.5), name)

            def sigmoid(x, ones, name):
                step(A(x, x, ACT.Exp, scale=-1.0))
                step(A(x, x, ACT.Ln, bias=ones))
                step(A(x, x, ACT.Exp, scale=-1.0), name)

            def squares(l, which):
                for k in range(KT):
                    if which == 0 and l == 0:
                        act.wait_ge(sem("x_turned"), k + 1)
                    elif which == 0:
                        need(act, "x_new", l - 1, 2 * KT, KT + k + 1)
                    else:
                        need(act, "x_new", l, 2 * KT, k + 1)
                    step(A(sq[:, k, :], xT[:, k, :], ACT.Square), "squared")

            def norm_stat(use, l):
                wait_filled(act, use, l)
                rsqrt_(l, rstd[:, :], bank(use, 0, T), D, name="rstd", use=use)

            act.wait_ge(sem("cols_ready"), 1)
            act.wait_ge(sem("c8"), 1)
            for l in range(DEPTH):
                squares(l, 0)
                wait_filled(act, "cpT", l)
                if l > 0:
                    need(act, "x_new", l - 1, 2 * KT)
                else:
                    act.wait_ge(sem("pre_filled"), KT)
                step(A(ckvT[:, 3 * P:7 * P], bank("cpT", 0, 512), ACT.Copy), bank_read=("cpT", l))
                norm_stat("ms1", l)
                for p in range(2):
                    wait_filled(act, f"ql{p}", l)
                    if p == 0:
                        need(act, "arena_b", l, 1)
                    step(A(qls[:, p, 0:T], bank(f"ql{p}", 0, T), ACT.Square), "qlat_sq")
                need(act, "kvr_ms", l, 1)
                step(A(small[:, 0:NT], small[:, 8:8 + NT], ACT.Ln, scale=1.0 / KVR, bias=eps_c[:, :]))
                step(A(small[:, 3:3 + NT], small[:, 11:11 + NT], ACT.Ln, scale=1.0 / ROPE, bias=eps_c[:, :]))
                step(A(small[:, 0:6], small[:, 0:6], ACT.Exp, scale=-0.5), "kvr_rstd")
                need(act, "gif_abs", l, 1)
                step(A(gl8[:, 0, :], gl8[:, 0, :], ACT.Exp, scale=-1.0))
                step(A(gl8[:, 0, :], gl8[:, 0, :], ACT.Ln, bias=one_c[0:8, :]), "gif_ln")
                for t in range(NT):
                    wait_filled(act, f"mv{t}", l)
                    step(A(vaug[:, t, :, 0:HD], bank(f"mv{t}", 0, G).rearrange("p (h e) -> p h e", h=H), ACT.Copy),
                         "vaug_d")
                    now_read(act, f"mv{t}")
                wait_filled(act, "cnT", l)
                step(A(ckvT[:, 0:3 * P], bank("cnT", 0, 3 * P), ACT.Copy), "ckvT")
                now_read(act, "cnT")
                wait_filled(act, "qms", l)
                rsqrt_(l, small[:, 16:16 + NT], bank("qms", 0, NT), QR, name="qlat_rstd", use="qms")
                need(act, "q_copied", l, 1)
                step(A(qsq[:, :, :, :].rearrange("p t h e -> p (t h e)"),
                       qtm[:, :, :, :].rearrange("p t h e -> p (t h e)"), ACT.Square), "q_squared")
                need(act, "q_ms", l, 1)
                step(A(small[:, 20:32], small[:, 44:56], ACT.Ln, scale=1.0 / HD, bias=eps_c[:, :]))
                step(A(small[:, 32:44], small[:, 56:68], ACT.Ln, scale=1.0 / ROPE, bias=eps_c[:, :]))
                step(A(small[:, 20:44], small[:, 20:44], ACT.Exp, scale=-0.5), "q_rstd")
                for p in range(2):
                    wait_filled(act, f"mk{p}", l)
                    step(A(kf[:, p, 0:T], bank(f"mk{p}", 0, T), ACT.Copy, scale=0.125), "mk_ready")
                    now_read(act, f"mk{p}")
                for i in range(KTILES):
                    u = f"kv{i}"
                    wait_filled(act, u, l)
                    kv = bank(u, 0, 512).rearrange("p (h e) -> p h e", h=H)
                    step(A(vb[:, i, :, :], kv[:, :, HD:], ACT.Copy), "vb_ready")
                    if i > 0:
                        need(act, "k_ms", l, KTILES, i)
                    step(A(ksq[:, :, :], kv[:, :, 0:HD], ACT.Square), "k_squared")
                need(act, "gate_arg", l, NT)
                sigmoid(gate[:, :, :].rearrange("p t n -> p (t n)"), one_c[:, :], "gate_d")
                need(act, "k_ms", l, KTILES)
                rsqrt_(l, small[:, 100:128], small[:, 72:100], HD, name="k_rstd")
                wait_filled(act, "rT", l)
                step(A(ctm[:, :, :].rearrange("p t h -> p (t h)"), bank("rT", 0, 12), ACT.Copy))
                step(A(em[:, :, :].rearrange("p t h -> p (t h)"), bank("rT", 12, 12), ACT.Exp), bank_read=("rT", l))
                wait_filled(act, "gx", l)
                step(A(glb[:, :], bank("gx", 0, H + 2 * DEC), ACT.Exp), "glb")
                now_read(act, "gx")
                wait_filled(act, "mkt", l)
                step(A(ktm[:, :, :].rearrange("p t n -> p (t n)"), bank("mkt", 0, NT * G), ACT.Copy), "ktm_d")
                now_read(act, "mkt")
                def raw_copy(n):
                    u = ("rq0", "rq1", "rk0", "rk1")[n]
                    wait_filled(act, u, l)
                    step(A(raws[n], bank(u, 0, T), ACT.Copy, scale=1.0 if n < 2 else 0.125), "raw_c")
                    now_read(act, u)

                def value_copy(t):
                    wait_filled(act, f"rv{t}", l)
                    step(A(vaug[:, t, :, 0:HD], bank(f"rv{t}", 0, G).rearrange("p (h e) -> p h e", h=H),
                           ACT.Copy), "vaug_c")
                    now_read(act, f"rv{t}")

                raw_copy(0)
                for h in range(H):
                    need(act, "dmx", l, H, h + 1)
                    d = dh[:, h % 2, :]
                    step(A(d[:, 0:256], dmx[:, 0:256], ACT.Exp, bias=ctm[:, 0, h:h + 1]))
                    step(A(d[:, 256:448], dmx[:, 256:448], ACT.Exp, bias=ctm[:, 1, h:h + 1]))
                    step(A(d[:, 448:512], dmx[:, 448:512], ACT.Exp, bias=ctm[:, 2, h:h + 1]), "decay_d")
                    if h > 0:
                        raw_copy(h)
                for h in range(H):
                    wait_filled(act, f"bk{h}", l)
                    if h > 0:
                        wait_filled(act, f"bs{h - 1}", l)
                    step(A(kT[0:QD, :], bank(f"bk{h}", 0, KTILES * P, QD), ACT.Copy), "kT")
                    now_read(act, f"bk{h}")
                    need(act, "probs_max", l, H, h + 1)
                    if h > 0:
                        wait_filled(act, f"bp{h - 1}", l)
                    for n, (a, w_) in enumerate(((0, 128), (128, 256), (448, 576))):
                        ins = A(pr[:, a:a + w_], bank(f"bs{h}", a, w_), ACT.Exp,
                                bias=small[:, 128 + 3 * h + n:129 + 3 * h + n],
                                accum_out=small[:, 140 + 3 * h + n:141 + 3 * h + n])
                        step(ins, "probs" if n == 2 else None)
                    now_read(act, f"bs{h}")
                    if h == 0:
                        need(act, "yms_d", l, 1)
                        rsqrt_(l, yst[:, 1, :], yst[:, 0, :], HD, name="yrstd_d")
                    if h == 1:
                        for t in range(NT):
                            need(act, "rg_arg", l, NT, t + 1)
                            sigmoid(gate[:, t, :], one_c[:, :], "rg_sig")
                    if h == 2:
                        value_copy(0)
                    if h == 3:
                        value_copy(1)
                        value_copy(2)
                        for u, a, n in (("rkt0", 0, 2), ("rkt1", 2, 1)):
                            wait_filled(act, u, l)
                            step(A(ktm[:, a:a + n, :].rearrange("p t n -> p (t n)"), bank(u, 0, n * G), ACT.Copy), "ktm_c")
                            now_read(act, u)
                    wait_filled(act, f"bp{h}", l)
                    if h > 0:
                        wait_filled(act, f"bo{h - 1}", l)
                    u = f"bp{h}"
                    step(A(pT[:, 0:384], bank(u, 0, 384), ACT.Copy))
                    step(A(pT[0:64, 384:512], bank(u, 384, 128, 64), ACT.Copy))
                    step(A(pT[:, 512:1024], bank(u, 512, 512), ACT.Copy), "pT")
                    now_read(act, u)
                need(act, "yms_b", l, 1)
                rsqrt_(l, yst[:, 4, :], yst[:, 3, :], HD, name="yrstd_b")
                for k in range(2):
                    if k == 0:
                        need(act, "mix1", l, 1)
                    step(A(xpad[:, k, 259:262], cols[:, ROWS["conv0"] + l * 6 + k:ROWS["conv0"] + l * 6 + k + 5:2], ACT.Copy))
                    wait_filled(act, f"lx{k}", l)
                    step(A(xpad[:, k, 3:259], bank(f"lx{k}", 0, SEQ), ACT.Copy))
                    step(A(xpad[:, k, 262:326], bank(f"lx{k}", SEQ, DEC), ACT.Copy), "xpad")
                    now_read(act, f"lx{k}")
                for k in range(2):
                    wait_filled(act, f"lg{k}", l)
                    step(A(lg[:, k, 0:SEQ], bank(f"lg{k}", 0, SEQ), ACT.Copy))
                    step(A(lg[:, k, AS:AW], bank(f"lg{k}", SEQ, DEC), ACT.Copy), "lg")
                    now_read(act, f"lg{k}")
                fl = lambda x: x[:, :, :].rearrange("p k n -> p (k n)")
                need(act, "yms_c", l, 1)
                rsqrt_(l, yst[:, 1, :], yst[:, 0, :], HD, name="yrstd_c")
                need(act, "gelu_arg", l, 1)
                sigmoid(fl(gg), one_c[:, :], "gelu_sig")
                need(act, "ri_arg", l, 4)
                sigmoid(ri[:, :, :, :].rearrange("p g k n -> p (g k n)"), one_c[:, :], "ri")
                need(act, "ay", l, 1)
                step(A(fl(aw), fl(ay), ACT.Exp), "aw")
                step(A(fl(an), fl(aw), ACT.Ln), "an")
                for t in range(2):
                    step(A(aa[:, t, :], ri[:, 0, t, :], ACT.Exp, scale=c8[:, 2 * l + t:2 * l + t + 1]))
                need(act, "ln_args", l, 1)
                step(A(fl(ln3), fl(ln3), ACT.Ln), "ln_done")
                need(act, "av", l, 1)
                step(A(fl(aw), fl(aw), ACT.Exp, scale=0.5), "au")
                need(act, "lru_scanned", l, 1)
                step(A(fl(an), fl(ah), ACT.Square), "h_sq")
                for t in range(2):
                    wait_filled(act, f"am{t}", l)
                    rsqrt_(l, aw[:, t, :], bank(f"am{t}", 0, AW), 1, name="a_rstd", use=f"am{t}")
                need(act, "x_new", l, 2 * KT, KT)
                squares(l, 1)
                norm_stat("ms2", l)
                for j in range(FT):
                    need(act, "fe_arg", l, FT, j + 1)
                    sigmoid(fe[:, j % 3, :], one_c[:, :], "fe")
            for t in range(NT):
                w = P if t < 2 else DEC
                for hf in range(2):
                    act.wait_ge(sem("y_turned"), 2 * t + hf + 1)
                    step(A(xtm[0:w, t, hf * 512:(hf + 1) * 512], ps[0:w, 2 * t + hf, :], ACT.Copy), "y_out")

        @block.vector
        def _(dve):
            step = stepper(dve, "dve_chain")
            v = nc.vector
            step(v.memset(eps_c[:, :], EPS), "eps_set")
            step(v.memset(one_c[:, :], 1.0), "eps_set")
            step(v.memset(xtm[DEC:P, 2, :], 0.0), "x_cleared")
            for t in (hT[:, :, T:TP], kf[:, :, T:TP], wt[:, :, 512:576], qg[:, :, DEC:P], r1[:, T:TP], nm[:, T:TP],
                      qh[:, :, :]):
                step(v.memset(t, 0.0))
            step(v.memset(vaug[:, :, :, HD:HD + 1], 1.0))
            for k in range(KT):
                dve.wait_ge(sem("pre_filled"), k + 1)
                step(v.tensor_copy(xT[:, k, :], ps[:, k, 0:T]), "x_turned")
            dve.wait_ge(sem("pre_filled"), KT + 1)
            step(v.tensor_copy(cols[:, :], ps[:, 0, 0:NROWS]), "cols_ready")
            dve.wait_ge(sem("pre_filled"), KT + 2)
            dve.wait_ge(sem("small_loaded"), 16 * NSMALL)
            for l in range(DEPTH):
                for p in range(2):
                    for a in range(2):
                        rs = slice(a * HD, (a + 1) * HD)
                        step(v.tensor_copy(ct[:, l, 2 * p + a, 0:HD],
                                           ps[:, 1, (2 * l + p) * P + a * HD:(2 * l + p) * P + (a + 1) * HD]))
            now_made(dve, "ct_ready")
            lam = cols[:, ROWS["lam"]:ROWS["lam"] + DEPTH * 2]
            step(v.scalar_tensor_tensor(out=lamt[:, 0, :], in0=lam, scalar=-1.0, in1=lam, op0=ALU.mult, op1=ALU.max), "lam_abs")
            step(v.memset(gq[:, :], SCALE))
            step(v.scalar_tensor_tensor(out=gq[0:HD, :], in0=cols[0:HD, ROWS["qn"]:ROWS["qn"] + DEPTH], scalar=SCALE,
                                        in1=cols[0:HD, ROWS["kn"]:ROWS["kn"] + DEPTH], op0=ALU.mult, op1=ALU.mult))
            dve.wait_ge(sem("lam_exp"), 1)
            z, s, s2, acc = (lamt[:, i, :] for i in (1, 0, 2, 3))
            step(v.tensor_scalar(s2, z, 2.0, None, ALU.add))
            step(v.reciprocal(acc, s2))
            step(v.tensor_tensor(s, z, acc, ALU.mult))
            step(v.tensor_tensor(s2, s, s, ALU.mult))
            step(v.memset(acc, 1.0 / 15))
            for n in (13, 11, 9, 7, 5, 3, 1):
                step(v.tensor_tensor(acc, acc, s2, ALU.mult))
                step(v.tensor_scalar(acc, acc, 1.0 / n, None, ALU.add))
            step(v.tensor_tensor(acc, acc, s, ALU.mult))
            step(v.tensor_scalar(s2, lam, -1.0, 0.0, ALU.mult, ALU.max))
            step(v.scalar_tensor_tensor(out=acc, in0=acc, scalar=2.0, in1=s2, op0=ALU.mult, op1=ALU.add))
            step(v.tensor_scalar(c8[:, :], acc, -LRU_C, None, ALU.mult))
            step(v.tensor_scalar(c16[:, :], acc, -2 * LRU_C, None, ALU.mult), "c8")

            def normalise(l, which, gain):
                need(dve, "rstd", l, 2, which + 1)
                for k in range(KT):
                    step(v.scalar_tensor_tensor(out=hT[:, k, 0:T], in0=xT[:, k, :], scalar=col(gain, l * KT + k),
                                                in1=rstd[:, :], op0=ALU.mult, op1=ALU.mult), "normed")

            def rope_t(x, out, heads):
                c2 = C("cos_t").rearrange("p (t n) -> p t n", t=NT)
                sn = C("sin_t").rearrange("p (t n) -> p t n", t=NT)
                if heads:
                    c2 = c2.unsqueeze(2).broadcast_to([P, NT, H, 32])
                    sn = sn.unsqueeze(2).broadcast_to([P, NT, H, 16])
                    lo, hi = (lambda a: a[:, :, :, 0:16]), (lambda a: a[:, :, :, 16:32])
                else:
                    lo, hi = (lambda a: a[:, :, 0:16]), (lambda a: a[:, :, 16:32])
                return c2, sn, lo, hi

            def group_tail(l, grp, y, stat):
                step(v.tensor_tensor(ysq[:, :, :, :].rearrange("p t h e -> p (t h) e"),
                                     y[:, :, :, :].rearrange("p t h e -> p (t h) e"),
                                     y[:, :, :, :].rearrange("p t h e -> p (t h) e"), ALU.mult))
                step(v.tensor_reduce(yst[:, stat, :], ysq[:, :, :, :].rearrange("p t h e -> p (t h) e"), AX.X, ALU.add),
                     f"yms_{grp}")

            def group_tail2(l, grp, y, stat, gate_):
                need(dve, f"yrstd_{grp}", l, 1)
                yv = y[:, :, :, :].rearrange("p t h e -> p (t h) e")
                step(v.tensor_tensor(yv, yv, yst[:, stat + 1, :].unsqueeze(2).broadcast_to([P, NT * H, HD]), ALU.mult),
                     None if gate_ else f"y_{grp}")
                if gate_:
                    step(v.tensor_tensor(yv, yv, gate[:, :, :].rearrange("p t (h e) -> p (t h) e", h=H), ALU.mult),
                         f"y_{grp}")

            def group_out(l, use, k0):
                wait_filled(dve, use, l)
                for p in range(2):
                    ins = v.tensor_scalar(mixT[:, k0 + p, :], bank(use, p * 512, T), col("out_norm", l * KT + k0 + p),
                                          None, ALU.mult)
                    if p == 0:
                        step(ins)
                    else:
                        step(ins, f"mix{k0 // 2}")
                now_read(dve, use)

            for l in range(DEPTH):
                if l == 0:
                    dve.wait_ge(sem("consts_loaded"), 16)
                normalise(l, 0, "norm_mix")
                for p in range(2):
                    if p == 0:
                        now_made(dve, "arena_b")
                    need(dve, "qlat_sq", l, 2, p + 1)
                    step(v.tensor_scalar(qlT[:, p, 0:T], bank(f"ql{p}", 0, T), col("q_norm", 2 * l + p), None, ALU.mult))
                    now_read(dve, f"ql{p}")
                step(v.memset(qlT[:, :, T:TP], 0.0), "qlat")
                step(v.memset(qls[:, :, T:TP], 0.0), "qlat")
                wait_filled(dve, "kvr", l)
                kvr = bank("kvr", 0, 480).rearrange("p (t n) -> p t n", t=NT)
                step(v.tensor_copy(ckvn[:, :, :], kvr[:, :, 0:KVR]))
                step(v.tensor_copy(krn[:, :, :], kvr[:, :, KVR:]), bank_read=("kvr", l))
                sc = ysq[:, :, :, :].rearrange("p t h e -> p t (h e)")
                step(v.tensor_tensor(sc[:, :, 0:KVR], ckvn[:, :, :], ckvn[:, :, :], ALU.mult))
                step(v.tensor_tensor(sc[:, :, KVR:KVR + ROPE], krn[:, :, :], krn[:, :, :], ALU.mult))
                step(v.tensor_reduce(small[:, 8:11], sc[:, :, 0:KVR], AX.X, ALU.add))
                step(v.tensor_reduce(small[:, 11:14], sc[:, :, KVR:KVR + ROPE], AX.X, ALU.add), "kvr_ms")
                need(dve, "kvr_rstd", l, 1)
                step(v.tensor_tensor(ckvn[:, :, :], ckvn[:, :, :],
                                     small[:, 0:3].unsqueeze(2).broadcast_to([P, NT, KVR]), ALU.mult))
                step(v.tensor_tensor(ckvn[:, :, :], ckvn[:, :, :],
                                     bcn[:, l, 0:KVR].unsqueeze(1).broadcast_to([P, NT, KVR]), ALU.mult), "ckv_new")
                wait_filled(dve, "mif", l)
                step(v.tensor_scalar(gif[:, :], bank("mif", 0, T, 8), col("b_if", l, 8), None, ALU.add), bank_read=("mif", l))
                step(v.scalar_tensor_tensor(out=gl8[:, 0, :], in0=gif[:, :], scalar=-1.0, in1=gif[:, :],
                                            op0=ALU.mult, op1=ALU.max), "gif_abs")
                step(v.tensor_tensor(krn[:, :, :], krn[:, :, :],
                                     small[:, 3:6].unsqueeze(2).broadcast_to([P, NT, ROPE]), ALU.mult))
                step(v.tensor_tensor(krn[:, :, :], krn[:, :, :],
                                     bcn[:, l, KVR:KVR + ROPE].unsqueeze(1).broadcast_to([P, NT, ROPE]), ALU.mult))
                c2, sn, lo, hi = rope_t(None, None, False)
                rt = sc[:, :, 0:32]
                step(v.tensor_tensor(lo(rt), hi(krn[:, :, :]), sn, ALU.mult))
                step(v.tensor_tensor(hi(rt), lo(krn[:, :, :]), sn, ALU.mult))
                step(v.tensor_tensor(krr[:, :, :], krn[:, :, :], c2, ALU.mult))
                step(v.tensor_tensor(lo(krr[:, :, :]), lo(krr[:, :, :]), lo(rt), ALU.subtract))
                step(v.tensor_tensor(hi(krr[:, :, :]), hi(krr[:, :, :]), hi(rt), ALU.add), "krope_new")
                need(dve, "gif_ln", l, 1)
                step(v.scalar_tensor_tensor(out=gl8[:, 0, :], in0=gif[:, :], scalar=0.0, in1=gl8[:, 0, :],
                                            op0=ALU.min, op1=ALU.subtract), "log_forget")
                for t in range(NT):
                    wait_filled(dve, f"mo{t}", l)
                    step(v.tensor_scalar(gate[:, t, :], bank(f"mo{t}", 0, G), SIG_MIN, None, ALU.max), "gate_arg")
                    now_read(dve, f"mo{t}")
                need(dve, "qlat_rstd", l, 1)
                for t in range(NT):
                    wait_filled(dve, f"qt{t}", l)
                    step(v.tensor_scalar(qtm[:, t, :, :].rearrange("p h e -> p (h e)"), bank(f"qt{t}", 0, H * QD),
                                         small[:, 16 + t:17 + t], None, ALU.mult), bank_read=(f"qt{t}", l))
                now_made(dve, "q_copied")
                wait_filled(dve, "lfr", l)
                step(v.tensor_copy(lfr[:, :], bank("lfr", 0, T, H)), bank_read=("lfr", l))
                one = C("ones", H)[:, 0:1]
                for a, e, init in ((0, SEQ, 0.0), (SEQ, T, m0[:, l:l + 1])):
                    step(v.tensor_tensor_scan(bro[:, a:e], C("ones", H)[:, 0:1].broadcast_to([H, e - a]), lfr[:, a:e],
                                              0.0, ALU.mult, ALU.add))
                    step(v.tensor_tensor_scan(mro[:, a:e], lfr[:, a:e], gif[0:H, a:e], init, ALU.add, ALU.max))
                step(v.tensor_tensor(r1[:, 0:T], gif[0:H, :], bro[:, :], ALU.subtract))
                step(v.tensor_tensor(r2[:, :], bro[:, :], mro[:, :], ALU.subtract))
                step(v.tensor_scalar(r3[:, :], r2[:, SEQ:T], m0[:, l:l + 1], None, ALU.add))
                step(v.tensor_scalar(nm[:, 0:T], mro[:, :], -1.0, None, ALU.mult), "m_rows")
                need(dve, "q_squared", l, 1)
                q12 = qtm[:, :, :, :].rearrange("p t h e -> p (t h) e")
                s12 = qsq[:, :, :, :].rearrange("p t h e -> p (t h) e")
                step(v.tensor_reduce(small[:, 44:56], s12[:, :, 0:HD], AX.X, ALU.add))
                step(v.tensor_reduce(small[:, 56:68], s12[:, :, HD:], AX.X, ALU.add), "q_ms")
                for p in range(2):
                    wait_filled(dve, f"mq{p}", l)
                    for a in range(2):
                        rs = slice(a * HD, (a + 1) * HD)
                        ins = v.tensor_copy(qh[rs, 2 * p + a, :], ps[rs, banks[f"mq{p}"][0], 0:T])
                        step(ins, "mq_ready" if a else None)
                    now_read(dve, f"mq{p}")
                need(dve, "q_rstd", l, 1)
                step(v.tensor_tensor(q12[:, :, 0:HD], q12[:, :, 0:HD],
                                     small[:, 20:32].unsqueeze(2).broadcast_to([P, 12, HD]), ALU.mult))
                step(v.tensor_tensor(q12[:, :, HD:], q12[:, :, HD:],
                                     small[:, 32:44].unsqueeze(2).broadcast_to([P, 12, ROPE]), ALU.mult))
                step(v.tensor_tensor(q12[:, :, HD:], q12[:, :, HD:],
                                     bcn[:, l, KVR + ROPE:].unsqueeze(1).broadcast_to([P, 12, ROPE]), ALU.mult))
                c2, sn, lo, hi = rope_t(None, None, True)
                x, tmp = qtm[:, :, :, HD:], qsq[:, :, :, 0:32]
                step(v.tensor_tensor(lo(tmp), hi(x), sn, ALU.mult))
                step(v.tensor_tensor(hi(tmp), lo(x), sn, ALU.mult))
                step(v.tensor_tensor(x, x, c2, ALU.mult))
                step(v.tensor_tensor(lo(x), lo(x), lo(tmp), ALU.subtract))
                step(v.tensor_tensor(hi(x), hi(x), hi(tmp), ALU.add), "q_ready")
                for i in range(KTILES):
                    need(dve, "k_squared", l, KTILES, i + 1)
                    step(v.tensor_copy(kb[:, i, :, 0:HD],
                                       bank(f"kv{i}", 0, 512).rearrange("p (h e) -> p h e", h=H)[:, :, 0:HD]),
                         bank_read=(f"kv{i}", l))
                    step(v.tensor_reduce(small[:, 72 + 4 * i:76 + 4 * i], ksq[:, :, :], AX.X, ALU.add), "k_ms")
                need(dve, "glb", l, 1)
                for p in range(2):
                    step(v.tensor_tensor(qg[:, 2 * p:2 * p + 2, 0:DEC], qh[:, 2 * p:2 * p + 2, SEQ:T],
                                         glb[:, H + p * DEC:H + (p + 1) * DEC].unsqueeze(1).broadcast_to([P, 2, DEC]),
                                         ALU.mult), "qg_d" if p else None)
                wait_bank_read(dve, "rT", l)

                def tails(h, src, e):
                    end = src[:, 255::128].unsqueeze(2).broadcast_to([P, NT, e])
                    return v.tensor_tensor(vw[:, h % 2, :, 0:e], vaug[:, :, h, 0:e], end, ALU.mult)

                def decay_arg(h):
                    wait_filled(dve, f"dd{h}", l)
                    step(v.tensor_tensor(dmx[:, :], bank(f"dd{h}", 0, 512), C("negmask"), ALU.add), "dmx")
                    now_read(dve, f"dd{h}")

                def d_out(h):
                    u = f"do{h}"
                    wait_filled(dve, u, l)
                    o = bank(u, 0, 195).rearrange("p (t e) -> p t e", t=NT)
                    rr = yst[:, 2, 0:3]
                    step(v.scalar_tensor_tensor(out=rr, in0=o[:, :, HD], scalar=-1.0, in1=em[:, :, h],
                                                op0=ALU.mult, op1=ALU.max))
                    step(v.tensor_tensor(rr, rr, o[:, :, HD], ALU.max))
                    step(v.reciprocal(rr, rr))
                    step(v.tensor_tensor(ytm[:, :, h, :], o[:, :, 0:HD], rr.unsqueeze(2).broadcast_to([P, NT, HD]), ALU.mult))
                    gstate = l * 2 * H + h
                    if gstate >= 2:
                        dve.wait_ge(sem("state_out"), gstate - 1)
                    step(v.tensor_copy(sst[:, h % 2, 0, :], bank(u, 200, 64, HD + 1)))
                    step(v.scalar_tensor_tensor(out=sst[:, h % 2, 1, :], in0=csn[:, l, h, :], scalar=glb[0:HD + 1, h:h + 1],
                                                in1=bank(u, 264, 64, HD + 1), op0=ALU.mult, op1=ALU.add), "state_d")
                    now_read(dve, u)

                need(dve, "vaug_d", l, 3)
                decay_arg(0)
                for i in range(KTILES):
                    src = krr[:, i, :] if i < 3 else pkr[:, l, i - 3, :]
                    step(v.tensor_copy(kb[:, i, :, HD:], src.unsqueeze(1).broadcast_to([P, H, ROPE])))
                need(dve, "k_rstd", l, 1)
                k28 = kb[:, :, :, :].rearrange("p k h e -> p (k h) e")
                step(v.tensor_tensor(k28[:, :, 0:HD], k28[:, :, 0:HD],
                                     small[:, 100:128].unsqueeze(2).broadcast_to([P, 28, HD]), ALU.mult), "kb_ready")
                for h in range(H):
                    need(dve, "decay_d", l, H, h + 1)
                    if h + 1 < H:
                        decay_arg(h + 1)
                    wait_filled(dve, f"ds{h}", l)
                    step(v.tensor_tensor(wt[:, h % 2, 0:512], bank(f"ds{h}", 0, 512), dh[:, h % 2, :], ALU.mult))
                    now_read(dve, f"ds{h}")
                    step(tails(h, dh[:, h % 2, :], HD + 1), "w_d")
                    if h > 0:
                        d_out(h - 1)
                d_out(H - 1)
                def rotate(n):
                    u = ("rqs0", "rqs1", "rks0", "rks1")[n]
                    p = n % 2
                    wait_filled(dve, u, l)
                    t2 = dmx[:, 0:T]
                    step(v.tensor_tensor(t2, bank(u, 0, T), C("sin_f"), ALU.mult), bank_read=(u, l))
                    step(v.tensor_tensor(raws[n], raws[n], C("cos_f"), ALU.mult))
                    if n < 2:
                        for a in range(2):
                            rs = slice(a * HD, (a + 1) * HD)
                            step(v.tensor_tensor(qh[rs, 2 * p + a, :], raws[n][rs], t2[rs], ALU.add),
                                 "rq_ready" if a else None)
                    else:
                        step(v.tensor_tensor(kf[:, p, 0:T], raws[n], t2, ALU.add), "rk_ready")

                def carry_c():
                    cr = C("cross").rearrange("p (k n) -> p k n", k=2)
                    for p in range(2):
                        step(v.tensor_tensor(qg[:, 2 * p:2 * p + 2, 0:DEC], qh[:, 2 * p:2 * p + 2, SEQ:T],
                                             cr[:, p, :].unsqueeze(1).broadcast_to([P, 2, DEC]), ALU.mult),
                             "qg_c" if p else None)

                for h in range(H):
                    if h == 1:
                        group_out(l, "dT", 6)
                    wait_filled(dve, f"bq{h}", l)
                    if h > 0:
                        wait_filled(dve, f"bs{h - 1}", l)
                    step(v.tensor_scalar(qT[0:QD, :], bank(f"bq{h}", 0, TP, QD), gq[0:QD, l:l + 1], None, ALU.mult), "qT")
                    now_read(dve, f"bq{h}")
                    if h == 0:
                        rotate(0)
                        rotate(1)
                    wait_filled(dve, f"bs{h}", l)
                    for n, (a, w_) in enumerate(((0, 128), (128, 256), (448, 576))):
                        step(v.tensor_reduce(small[:, 128 + 3 * h + n:129 + 3 * h + n], bank(f"bs{h}", a, w_), AX.X, ALU.max,
                                             negate=True), "probs_max" if n == 2 else None)
                    if h == 0:
                        group_tail(l, "d", ytm, 0)
                        need(dve, "gate_d", l, 1)
                        group_tail2(l, "d", ytm, 0, True)
                    if h == 1:
                        for t in range(NT + 1):
                            if t < NT:
                                wait_filled(dve, f"rg{t}", l)
                                step(v.tensor_scalar(gate[:, t, :], bank(f"rg{t}", 0, G), SIG_MIN, None, ALU.max), "rg_arg")
                            if t > 0:
                                need(dve, "rg_sig", l, NT, t)
                                step(v.tensor_tensor(gate[:, t - 1, :], gate[:, t - 1, :], bank(f"rg{t - 1}", 0, G),
                                                     ALU.mult), bank_read=(f"rg{t - 1}", l))
                    if h == 2:
                        rotate(2)
                        rotate(3)
                        carry_c()
                    need(dve, "probs", l, H, h + 1)
                    rs3 = small[:, 152 + 3 * h:155 + 3 * h]
                    step(v.reciprocal(rs3, small[:, 140 + 3 * h:143 + 3 * h]))
                    wait_filled(dve, f"bo{h}", l)
                    step(v.tensor_tensor(ybm[:, :, h, :], bank(f"bo{h}", 0, 192).rearrange("p (t e) -> p t e", t=NT),
                                         rs3.unsqueeze(2).broadcast_to([P, NT, HD]), ALU.mult), bank_read=(f"bo{h}", l))
                group_tail(l, "b", ybm, 3)
                dec = C("decay").rearrange("p (h n) -> p h n", h=H)
                need(dve, "vaug_c", l, 3)

                def c_out(h):
                    u = f"co{h}"
                    wait_filled(dve, u, l)
                    step(v.tensor_copy(ytm[:, :, h, :], bank(u, 0, 192).rearrange("p (t e) -> p t e", t=NT)))
                    dve.wait_ge(sem("state_out"), l * 2 * H + H + h - 1)
                    step(v.tensor_copy(sst[0:HD, h % 2, 0, :], bank(u, 200, 64, HD)))
                    step(v.scalar_tensor_tensor(out=sst[0:HD, h % 2, 1, :], in0=s0n[:, l, h, :],
                                                scalar=float(np.exp(DEC * LG[h])),
                                                in1=bank(u, 264, 64, HD), op0=ALU.mult, op1=ALU.add), "state_c")
                    now_read(dve, u)

                for h in range(H):
                    step(tails(h, dec[:, h, :], HD))
                    wait_filled(dve, f"cs{h}", l)
                    step(v.tensor_tensor(wt[:, h % 2, 0:512], bank(f"cs{h}", 0, 512), dec[:, h, :], ALU.mult), "w_c")
                    now_read(dve, f"cs{h}")
                    if h == 0:
                        group_tail2(l, "b", ybm, 3, False)
                    if h > 0:
                        c_out(h - 1)
                    if h == 1:
                        dve.wait_ge(sem("b_out"), l + 1)
                        group_out(l, "bT", 2)
                c_out(H - 1)
                for k in range(2):
                    step(v.memset(xpad[:, k, 0:3], 0.0))
                    need(dve, "xpad", l, 2, k + 1)
                    wj = lambda j: col("conv_w", l * 8 + j * 2 + k)
                    step(v.tensor_scalar(xc[:, k, :], xpad[:, k, 0:AW], wj(0), col("conv_b", 2 * l + k), ALU.mult, ALU.add))
                    for j in range(1, CONV):
                        step(v.scalar_tensor_tensor(out=xc[:, k, :], in0=xpad[:, k, j:j + AW], scalar=wj(j), in1=xc[:, k, :],
                                                    op0=ALU.mult, op1=ALU.add), "conv_done" if (k == 1 and j == 3) else None)
                now_made(dve, "lru_x_in")
                group_tail(l, "c", ytm, 0)
                for k in range(2):
                    need(dve, "lg", l, 2, k + 1)
                step(v.memset(lg[:, :, SEQ:AS], 0.0))
                fl = lambda x: x[:, :, :].rearrange("p k n -> p (k n)")
                step(v.tensor_tensor(fl(gg), fl(lg), fl(lg), ALU.mult))
                step(v.tensor_scalar(fl(gg), fl(gg), 0.044715, 1.0, ALU.mult, ALU.add))
                step(v.scalar_tensor_tensor(out=fl(gg), in0=fl(gg), scalar=GELU, in1=fl(lg), op0=ALU.mult, op1=ALU.mult))
                step(v.tensor_scalar(fl(gg), fl(gg), SIG_MIN, None, ALU.max), "gelu_arg")
                for t in range(2):
                    for g_, u in enumerate((f"ga{t}", f"gx{t}_")):
                        wait_filled(dve, u, l)
                        step(v.tensor_scalar(ri[:, g_, t, :], bank(u, 0, AW), col(("ba", "bx")[g_], 2 * l + t), SIG_MIN,
                                             ALU.add, ALU.max), "ri_arg")
                        now_read(dve, u)
                group_tail2(l, "c", ytm, 0, True)
                need(dve, "gelu_sig", l, 1)
                step(v.tensor_tensor(fl(gg), fl(gg), fl(lg), ALU.mult))
                group_out(l, "cT", 4)
                need(dve, "ri", l, 1)
                for t in range(2):
                    step(v.tensor_scalar(ay[:, t, :], ri[:, 0, t, :], c16[:, 2 * l + t:2 * l + t + 1], -41.5, ALU.mult, ALU.max),
                         "ay" if t else None)
                step(v.tensor_scalar(ln3[:, 2, :], fl(ay), -1.0, LN_MIN, ALU.mult, ALU.max))
                fi = ri[:, 1, :, :].rearrange("p k n -> p (k n)")
                step(v.tensor_tensor(fi, fi, fl(xc), ALU.mult))
                need(dve, "aw", l, 1)
                step(v.tensor_scalar(ln3[:, 0, :], fl(aw), -1.0, 1.0, ALU.mult, ALU.add))
                step(v.tensor_scalar(ln3[:, 0, :], ln3[:, 0, :], LN_MIN, None, ALU.max))
                need(dve, "an", l, 1)
                step(v.tensor_scalar(ln3[:, 1, :], fl(an), -1.0, LN_MIN, ALU.mult, ALU.max), "ln_args")
                need(dve, "ln_done", l, 1)
                step(v.tensor_tensor(fl(aw), ln3[:, 0, :], ln3[:, 1, :], ALU.subtract))
                step(v.tensor_tensor(fl(aw), fl(aw), ln3[:, 2, :], ALU.add), "av")
                need(dve, "au", l, 1)
                step(v.tensor_tensor(fl(ay), fi, fl(aw), ALU.mult))
                step(v.memset(ah[:, :, SEQ:AS], 0.0))
                for k in range(2):
                    step(v.tensor_tensor_scan(ah[:, k, 0:SEQ], aa[:, k, 0:SEQ], ay[:, k, 0:SEQ], 0.0, ALU.mult, ALU.add))
                    step(v.tensor_tensor_scan(ah[:, k, AS:AW], aa[:, k, AS:AW], ay[:, k, AS:AW], col("h0", 2 * l + k),
                                              ALU.mult, ALU.add), "lru_scanned" if k else None)
                for k in range(2):
                    step(v.scalar_tensor_tensor(out=gg[:, k, :], in0=gg[:, k, :], scalar=col("out_norm", l * KT + k),
                                                in1=ah[:, k, :], op0=ALU.mult, op1=ALU.mult))
                for k in range(2):
                    need(dve, "a_rstd", l, 2, k + 1)
                    step(v.tensor_tensor(mixT[:, k, 0:SEQ], gg[:, k, 0:SEQ], aw[:, k, 0:SEQ], ALU.mult))
                    step(v.tensor_tensor(mixT[:, k, SEQ:T], gg[:, k, AS:AW], aw[:, k, AS:AW], ALU.mult),
                         "mix0" if k else None)
                for n in range(KT):
                    wait_filled(dve, f"o{n}", l)
                    step(v.tensor_tensor(xT[:, n, :], xT[:, n, :], bank(f"o{n}", 0, T), ALU.add), "x_new")
                    now_read(dve, f"o{n}")
                normalise(l, 1, "norm_ffn")
                dve.wait_ge(sem("a_out"), l + 1)

                def gate_arg(j):
                    wait_filled(dve, f"fg{j}", l)
                    step(v.tensor_scalar(fe[:, j % 3, :], bank(f"fg{j}", 0, T), SIG_MIN, None, ALU.max), "fe_arg")

                for j in range(FT):
                    if j == 0:
                        gate_arg(0)
                    if j + 1 < FT:
                        gate_arg(j + 1)
                    need(dve, "fe", l, FT, j + 1)
                    e = fe[:, j % 3, :]
                    step(v.tensor_tensor(fs, e, bank(f"fg{j}", 0, T), ALU.mult), bank_read=(f"fg{j}", l))
                    wait_filled(dve, f"fu{j}", l)
                    step(v.tensor_tensor(aT[:, j, :], fs, bank(f"fu{j}", 0, T), ALU.mult), "hidden")
                    now_read(dve, f"fu{j}")
                for n in range(KT):
                    wait_filled(dve, f"y{n}", l)
                    step(v.tensor_tensor(xT[:, n, :], xT[:, n, :], bank(f"y{n}", 0, T), ALU.add), "x_new")
                    now_read(dve, f"y{n}")
        for k, n in per.items():
            assert made.get(k, 0) == n * DEPTH, (k, made.get(k), n)
        return len(sems)


_INS = ["x_prompt", "x_sample", "cache_mla_ckv", "cache_mla_krope", "state_lru_h", "state_lru_conv",
        "state_ret", "state_mlstm_C", "state_mlstm_n", "state_mlstm_m",
        "norm_mix", "w_in", "lru_conv_w", "lru_conv_b", "lru_wa", "lru_ba", "lru_wx", "lru_bx", "lru_lambda",
        "mla_q_norm", "mla_wq_b", "mla_qn_norm", "mla_qr_norm", "mla_kv_norm", "mla_kr_norm", "mla_wkv_b",
        "mla_kn_norm", "mlstm_b_if", "out_norm", "w_out", "norm_ffn", "w_gu", "w_down"]
_STATES = [("ckv", lambda t: (t, KVR)), ("krope", lambda t: (t, ROPE)), ("lru_h", lambda t: (G,)),
           ("lru_conv", lambda t: (CONV - 1, G)), ("ret", lambda t: (H, HD, HD)),
           ("mC", lambda t: (H, HD, HD)), ("mn", lambda t: (H, HD)), ("mm", lambda t: (H,))]
_OUTS = [("yp", (1, SEQ, D)), ("ys", (1, DEC, D))]
_OUTS += [(f"{s}_{n}", (DEPTH, 1) + f(t)) for s, t in (("p", SEQ), ("s", DEC)) for n, f in _STATES]


def kernel(**inputs):
    import numpy as _np
    import concourse.bacc as _bacc
    from concourse import mybir as _mybir
    from concourse.bass_utils import run_bass_kernel_spmd as _run

    nc = _bacc.Bacc("TRN2", target_bir_lowering=False, num_devices=1)
    arrays, ins, outs = {}, {}, {}
    for name in _INS:
        a = _np.ascontiguousarray(inputs[name])
        arrays[f"in_{name}"] = a
        ins[name] = nc.dram_tensor(f"in_{name}", a.shape, _mybir.dt.from_np(a.dtype), kind="ExternalInput").ap()
    tables = constants()[0]
    arrays["in_consts"] = tables
    ins["consts"] = nc.dram_tensor("in_consts", tables.shape, _mybir.dt.float32, kind="ExternalInput").ap()
    for name, shape in _OUTS:
        outs[name] = nc.dram_tensor(f"out_{name}", shape, _mybir.dt.float32, kind="ExternalOutput").ap()
    build(nc, ins, outs)
    r = _run(nc, [arrays], core_ids=[0])
    return tuple(r.results[0][f"out_{name}"] for name, _ in _OUTS)
```
